# Optimizing a Trainium2 kernel written in Bass

```python
import jax, jax.numpy as jnp
from jax import lax
import numpy as np

D_MODEL = 1024
BATCH = 1
SEQ = 256
DEPTH = 2

HEAD_DIM = 128
A_HEADS = D_MODEL // HEAD_DIM
B_HEADS = D_MODEL // HEAD_DIM
HGRN_CHUNK = 64
MOBA_BLOCK = 256
MOBA_TOPK = 3
MOBA_QCHUNK = 16
D_FF = ((8 * D_MODEL // 3 + 255) // 256) * 256
N_EXPERTS = 8
MOE_TOPK = 2
D_FF_EXPERT = 7 * D_MODEL // 2
N_A = DEPTH // 2
N_B = DEPTH - N_A
N_DENSE = (DEPTH + 1) // 2
N_MOE = DEPTH // 2
EPS = 1e-6

kernel_name = "yoco_hgrn2_moba_moe_trunk"

def rmsnorm(x, g):
    xf = x.astype(jnp.float32)
    y = xf * lax.rsqrt(jnp.mean(xf * xf, axis=-1, keepdims=True) + EPS)
    return (y * g.astype(jnp.float32)).astype(x.dtype)

def alibi_slopes(n_heads):
    return jnp.asarray(2.0 ** (-8.0 * np.arange(1, n_heads + 1) / n_heads), dtype=jnp.float32)

def hgrn2_mixer(h, w_in, lb, out_gain, w_o):
    B, S, D = h.shape
    H, dk, C = A_HEADS, HEAD_DIM, HGRN_CHUNK
    NC = S // C
    q, fz, i_in, g = jnp.split(h @ w_in, 4, axis=-1)
    q = jax.nn.silu(q.astype(jnp.float32))
    fz = fz.astype(jnp.float32)
    v = i_in.astype(jnp.float32)
    lb = lb.astype(jnp.float32)
    log_f = jnp.logaddexp(jnp.log(lb), jnp.log1p(-lb) + jax.nn.log_sigmoid(fz))
    k = (1.0 - lb) * jax.nn.sigmoid(-fz)

    def to_chunks(t):
        return t.reshape(B, NC, C, H, dk).transpose(0, 3, 1, 2, 4)

    q, k, v, log_f = to_chunks(q), to_chunks(k), to_chunks(v), to_chunks(log_f)
    b = jnp.cumsum(log_f, axis=3)
    b_ref = b[:, :, :, C // 2 - 1:C // 2, :]
    b_last = b[:, :, :, -1:, :]
    a = jnp.einsum('bhnid,bhnjd->bhnij', q * jnp.exp(b - b_ref), k * jnp.exp(b_ref - b))
    causal = jnp.tril(jnp.ones((C, C), dtype=bool))
    a = jnp.where(causal, a, 0.0)
    o = jnp.einsum('bhnij,bhnjv->bhniv', a, v)
    ds = jnp.einsum('bhnjd,bhnjv->nbhdv', k * jnp.exp(b_last - b), v)
    decay = jnp.exp(b_last[:, :, :, 0, :]).transpose(2, 0, 1, 3)

    def step(state, inp):
        dec, d_s = inp
        return dec[..., None] * state + d_s, state

    _, s_prev = lax.scan(step, jnp.zeros((B, H, dk, dk), jnp.float32), (decay, ds))
    o = o + jnp.einsum('bhnid,nbhdv->bhniv', q * jnp.exp(b), s_prev)
    o = o * lax.rsqrt(jnp.mean(o * o, axis=-1, keepdims=True) + EPS)
    o = o.transpose(0, 2, 3, 1, 4).reshape(B, S, D)
    o = o * out_gain.astype(jnp.float32) * jax.nn.silu(g.astype(jnp.float32))
    return o.astype(h.dtype) @ w_o

def shared_kv(x, g, w_kv):
    B, S, D = x.shape
    H, dh, BS = B_HEADS, HEAD_DIM, MOBA_BLOCK
    nb = -(-S // BS)
    s_pad = nb * BS
    k, v = jnp.split(rmsnorm(x, g) @ w_kv, 2, axis=-1)

    def heads(t):
        t = t.reshape(B, S, H, dh).transpose(0, 2, 1, 3)
        return jnp.pad(t, ((0, 0), (0, 0), (0, s_pad - S), (0, 0)))

    k, v = heads(k), heads(v)
    k_mean = jnp.mean(k.reshape(B, H, nb, BS, dh).astype(jnp.float32), axis=3)
    return k, v, k_mean

def moba_mixer(h, w_q, w_o, k_pad, v_pad, k_mean):
    B, S, D = h.shape
    H, dh, BS, QC = B_HEADS, HEAD_DIM, MOBA_BLOCK, MOBA_QCHUNK
    nb = k_mean.shape[2]
    scale = HEAD_DIM ** -0.5
    q = (h @ w_q).reshape(B, S, H, dh).transpose(0, 2, 1, 3)
    pos = jnp.arange(S)
    q_blk = pos // BS
    gate = jnp.einsum('bhsd,bhnd->bhsn', q.astype(jnp.float32), k_mean)
    past = jnp.arange(nb)[None, :] < q_blk[:, None]
    gate = jnp.where(past, gate, -jnp.inf)
    kk = min(MOBA_TOPK, nb)
    _, sel = lax.top_k(gate, kk)
    valid = jnp.arange(kk)[None, :] < q_blk[:, None]
    k_blocks = k_pad.reshape(B, H, nb, BS, dh)
    v_blocks = v_pad.reshape(B, H, nb, BS, dh)
    slopes = alibi_slopes(H)
    b_idx = jnp.arange(B)[:, None, None]
    h_idx = jnp.arange(H)[None, :, None]
    r = jnp.arange(BS)

    def attend_chunk(c):
        start = c * QC
        qc = lax.dynamic_slice_in_dim(q, start, QC, axis=2)
        selc = lax.dynamic_slice_in_dim(sel, start, QC, axis=2)
        validc = lax.dynamic_slice_in_dim(valid, start, QC, axis=0)
        tq = start + jnp.arange(QC)
        own_start = (start // BS) * BS
        k_own = lax.dynamic_slice_in_dim(k_pad, own_start, BS, axis=2)
        v_own = lax.dynamic_slice_in_dim(v_pad, own_start, BS, axis=2)
        dist_own = tq[:, None] - (own_start + r)[None, :]
        s_own = (jnp.einsum('bhqd,bhrd->bhqr', qc, k_own).astype(jnp.float32) * scale
                 - slopes[:, None, None] * dist_own)
        scores = [jnp.where(dist_own >= 0, s_own, -jnp.inf)]
        for i in range(kk):
            blk = selc[..., i]
            kg = k_blocks[b_idx, h_idx, blk]
            dist = tq[:, None] - (blk[..., None] * BS + r)
            s = (jnp.einsum('bhqd,bhqrd->bhqr', qc, kg).astype(jnp.float32) * scale
                 - slopes[None, :, None, None] * dist)
            scores.append(jnp.where(validc[:, i][None, None, :, None], s, -jnp.inf))
        p = jax.nn.softmax(jnp.concatenate(scores, axis=-1), axis=-1).astype(v_pad.dtype)
        p = p.reshape(B, H, QC, kk + 1, BS)
        out = jnp.einsum('bhqr,bhrd->bhqd', p[:, :, :, 0], v_own)
        for i in range(kk):
            vg = v_blocks[b_idx, h_idx, selc[..., i]]
            out = out + jnp.einsum('bhqr,bhqrd->bhqd', p[:, :, :, i + 1], vg)
        return out

    outs = lax.map(attend_chunk, jnp.arange(S // QC))
    o = outs.transpose(1, 0, 3, 2, 4).reshape(B, S, D)
    return o @ w_o

def swiglu(h, w_gu, w_down):
    gte, up = jnp.split(h @ w_gu, 2, axis=-1)
    return (jax.nn.silu(gte) * up) @ w_down

def moe_ffn(h, w_router, w_gu, w_down):
    B, S, D = h.shape
    hf = h.reshape(B * S, D)
    logits = (hf @ w_router).astype(jnp.float32)
    top_vals, top_idx = lax.top_k(logits, MOE_TOPK)
    top_w = jax.nn.softmax(top_vals, axis=-1)
    gates = jnp.sum(jax.nn.one_hot(top_idx, N_EXPERTS, dtype=jnp.float32) * top_w[..., None], axis=1)
    gates = gates.astype(h.dtype)
    y = jnp.zeros_like(hf)
    for e in range(N_EXPERTS):
        y = y + gates[:, e:e + 1] * swiglu(hf, w_gu[e], w_down[e])
    return y.reshape(B, S, D)

def setup_inputs(seed: int = 0) -> dict:
    key = jax.random.key(seed)
    ks = jax.random.split(key, 20)
    f32 = jnp.float32

    def dense(k, shape, fan_in):
        return jax.random.normal(k, shape, f32) * (fan_in ** -0.5)

    def gain(k, shape):
        return 1.0 + 0.02 * jax.random.normal(k, shape, f32)

    D = D_MODEL
    return {
        "x": jax.random.normal(ks[0], (BATCH, SEQ, D), f32),
        "attn_norm": gain(ks[1], (DEPTH, D)),
        "ffn_norm": gain(ks[2], (DEPTH, D)),
        "hgrn_w_in": dense(ks[3], (N_A, D, 4 * D), D),
        "hgrn_lb_logits": jax.random.normal(ks[4], (N_A, D), f32),
        "hgrn_out_norm": gain(ks[5], (N_A, D)),
        "hgrn_w_o": dense(ks[6], (N_A, D, D), D),
        "kv_norm": gain(ks[7], (D,)),
        "w_kv": dense(ks[8], (D, 2 * D), D),
        "moba_w_q": dense(ks[9], (N_B, D, D), D),
        "moba_w_o": dense(ks[10], (N_B, D, D), D),
        "ffn_w_gu": dense(ks[11], (N_DENSE, D, 2 * D_FF), D),
        "ffn_w_down": dense(ks[12], (N_DENSE, D_FF, D), D_FF),
        "moe_router": dense(ks[13], (N_MOE, D, N_EXPERTS), D),
        "moe_w_gu": dense(ks[14], (N_MOE, N_EXPERTS, D, 2 * D_FF_EXPERT), D),
        "moe_w_down": dense(ks[15], (N_MOE, N_EXPERTS, D_FF_EXPERT, D), D_FF_EXPERT),
        "final_norm": gain(ks[16], (D,)),
    }

def reference(x, attn_norm, ffn_norm, hgrn_w_in, hgrn_lb_logits, hgrn_out_norm, hgrn_w_o,
              kv_norm, w_kv, moba_w_q, moba_w_o, ffn_w_gu, ffn_w_down,
              moe_router, moe_w_gu, moe_w_down, final_norm):
    lb_p = jax.nn.softmax(hgrn_lb_logits.astype(jnp.float32), axis=0)
    lb_cum = jnp.cumsum(lb_p, axis=0)
    lower_bounds = lb_cum - lb_cum[:1]
    k_pad = v_pad = k_mean = None
    for layer in range(DEPTH):
        h = rmsnorm(x, attn_norm[layer])
        if layer < N_A:
            x = x + hgrn2_mixer(h, hgrn_w_in[layer], lower_bounds[layer],
                                hgrn_out_norm[layer], hgrn_w_o[layer])
        else:
            if layer == N_A:
                k_pad, v_pad, k_mean = shared_kv(x, kv_norm, w_kv)
            j = layer - N_A
            x = x + moba_mixer(h, moba_w_q[j], moba_w_o[j], k_pad, v_pad, k_mean)
        h = rmsnorm(x, ffn_norm[layer])
        if layer % 2 == 0:
            x = x + swiglu(h, ffn_w_gu[layer // 2], ffn_w_down[layer // 2])
        else:
            x = x + moe_ffn(h, moe_router[layer // 2], moe_w_gu[layer // 2], moe_w_down[layer // 2])
    return rmsnorm(x, final_norm)


_drawn_inputs = setup_inputs


def setup_inputs(seed=0):
    import zlib

    import numpy as np

    out = dict(_drawn_inputs(seed))
    spreads = {}
    factors = {}
    for name, (base, spread) in spreads.items():
        noise = np.random.default_rng([zlib.crc32(name.encode()), seed]).standard_normal(out[name].shape)
        drawn = base * np.exp(spread * noise) if base else spread * noise
        out[name] = __import__('jax').numpy.asarray(drawn.astype(out[name].dtype))
    for name, factor in factors.items():
        out[name] = (out[name] * factor).astype(out[name].dtype)
    return out
```

```python
from contextlib import ExitStack

import numpy as np
import concourse.bass as bass
from concourse import mybir

F32 = mybir.dt.float32
F32R = mybir.dt.float32r
I32 = mybir.dt.int32
U32 = mybir.dt.uint32
ACT = mybir.ActivationFunctionType
ALU = mybir.AluOpType
AX_X = mybir.AxisListType.X

P = 128
EPS = 1e-6
RAW_SLOTS = 6
SPLIT_SLOTS = 3
PANEL = 2048


def build_trunk(nc, x, attn_norm, ffn_norm, hgrn_w_in, hgrn_lb_logits, hgrn_out_norm, hgrn_w_o,
                kv_norm, w_kv, moba_w_q, moba_w_o, ffn_w_gu, ffn_w_down,
                moe_router, moe_w_gu, moe_w_down, final_norm, out):
    _, S, D = x.shape
    TT = S // P
    KT = D // P
    H = KT
    CH = 64
    NCH = S // CH
    F = ffn_w_down.shape[1]
    E = moe_w_gu.shape[1]
    FE = moe_w_down.shape[2]
    FG = F // 256
    EG = FE // 512
    SCALE = float(P) ** -0.5
    SLOPES = [2.0 ** (-8.0 * (h + 1) / H) for h in range(H)]
    assert hgrn_w_in.shape[0] == 1 and moba_w_q.shape[0] == 1 and S == 256 and H == 8 and TT == 2
    EXTRA = (2 * S - E) // P
    EXTRA = min(EXTRA, 2 * S // (P + 1))
    NPASS = E + EXTRA

    def halves(v):
        k = v.shape[1] // 2
        return [("k", v[:, 0:k, :]), ("k", v[:, k:2 * k, :])]

    def square(w, c0, kh):
        return halves(w[kh * 512:(kh + 1) * 512, c0:c0 + 512].rearrange("(k p) c -> p k c", p=P))

    dense = []
    for c0 in (D, D + 512, 0, 512, 2 * D, 2 * D + 512, 3 * D, 3 * D + 512):
        dense += [square(hgrn_w_in[0], c0, kh) for kh in range(2)]
    AT_WO = len(dense)
    for c0 in (0, 512):
        dense += [square(hgrn_w_o[0], c0, kh) for kh in range(2)]
    AT_FFN = len(dense)
    gu_view = ffn_w_gu[0].rearrange("(k p) (u f) -> p k u f", p=P, u=2)
    down_view = ffn_w_down[0].rearrange("(k p) c -> p k c", p=P)
    ffn_order = [("G", 0)]
    for j in range(1, FG):
        ffn_order += [("G", j), ("D", j - 1)]
    ffn_order += [("D", FG - 1)]
    ffn_panels = []
    for kind, j in ffn_order:
        if kind == "G":
            for kh in range(2):
                dense.append([("u", gu_view[:, 4 * kh:4 * kh + 4, u, j * 256:(j + 1) * 256]) for u in range(2)])
                ffn_panels.append((kind, j, kh))
        else:
            dense.append(halves(down_view[:, 2 * j:2 * j + 2, :]))
            ffn_panels.append((kind, j, 0))
    AT_Q = len(dense)
    for w, c0 in ((moba_w_q[0], 0), (w_kv, 0), (w_kv, D)):
        for c in (c0, c0 + 512):
            dense += [square(w, c, kh) for kh in range(2)]
    AT_KV = AT_Q + 4
    AT_WO2 = len(dense)
    for c0 in (0, 512):
        dense += [square(moba_w_o[0], c0, kh) for kh in range(2)]
    MOE0 = len(dense)
    order = [("G", 0)]
    for j in range(1, EG):
        order += [("G", j), ("D", j - 1)]
    order += [("D", EG - 1)]
    moe_panels = [(k, j, m) for k, j in order for m in range(4 if k == "G" else 2)]
    NP = len(moe_panels)
    ffn_end = {(k, j): n + 1 for n, (k, j, _) in enumerate(ffn_panels)}
    moe_end = {(k, j): n + 1 for n, (k, j, _) in enumerate(moe_panels)}
    assert NP % RAW_SLOTS == 0 and NP % SPLIT_SLOTS == 0

    GR_IN, GR_WO = 0, 8
    GR_FFN = GR_WO + 2
    GR_Q = GR_FFN + FG
    GR_WO2 = GR_Q + 6
    GROUPS = GR_WO2 + 2

    ctx = ExitStack()
    with ctx:
        def sb(name, shape, dt=F32):
            return ctx.enter_context(nc.sbuf_tensor(name, shape, dt))

        def sem(name):
            return ctx.enter_context(nc.semaphore(name))

        w_raw = sb("w_raw", [P, RAW_SLOTS, PANEL])
        w_hi = sb("w_hi", [P, SPLIT_SLOTS, PANEL], F32R)
        w_lo = sb("w_lo", [P, SPLIT_SLOTS, PANEL], F32R)
        h_hi = sb("h_hi", [P, KT, S], F32R)
        h_lo = sb("h_lo", [P, KT, S], F32R)
        a_hi = sb("a_hi", [P, 2, 512], F32R)
        a_lo = sb("a_lo", [P, 2, 512], F32R)
        x_res = sb("x_res", [P, TT, D])
        junk = sb("junk", [P, D])
        work = [sb(f"work{n}", [P, 2048]) for n in range(8)]
        qT, kT, zT, tT = work[0], work[1], work[2], work[3]
        v_tm, g_tm = work[4], work[5]
        xn = work[6]
        ident = sb("ident", [P, P])
        chunk_mask = sb("chunk_mask", [P, P])
        earlier = sb("earlier", [P, P])
        ones = sb("ones", [P, P])
        slot_id = sb("slot_id", [P, P])
        expert_id = sb("expert_id", [P, E])
        alibi = sb("alibi", [P, 3 * P])
        scan_keep = sb("scan_keep", [P, NCH, CH])
        gain_rows = sb("gain_rows", [6 * KT, P])
        gains = sb("gains", [P, 6 * KT])
        router = sb("router", [P, KT, E])
        sumsq = sb("sumsq", [P, 5, TT])
        mean_sq = sb("mean_sq", [P, 5, TT])
        std = sb("std", [P, 5, TT])
        rstd = sb("rstd", [P, 5, TT])
        b_ref = sb("b_ref", [P, H, NCH])
        b_last = sb("b_last", [P, H, NCH])
        alpha = sb("alpha", [P, H, NCH])
        head_ms = sb("head_ms", [P, TT, H])
        head_std = sb("head_std", [P, TT, H])
        head_rstd = sb("head_rstd", [P, TT, H])
        soft = sb("soft", [P, H, 8])
        sel = sb("sel", [P, TT, P])
        sel_T = sb("sel_T", [P, S])
        route = sb("route", [P, TT, 12, 8])
        route_u = sb("route_u", [P, TT, 8], U32)
        pass_rank = sb("pass_rank", [P, TT, NPASS + 2])
        pass_gate = sb("pass_gate", [P, TT, NPASS + 2])
        over = sb("over", [P, 8, 8])
        info_f = sb("info_f", [P, 4])
        info = sb("info", [P, 4], I32)
        ps = ctx.enter_context(nc.psum_tensor("ps", [P, 8, 512], F32))

        GAIN_ATTN0, GAIN_ATTN1, GAIN_FFN0, GAIN_FFN1, GAIN_OUT, GAIN_KV = (n * KT for n in range(6))

        raw_landed = [sem(f"raw_landed{s}") for s in range(RAW_SLOTS)]
        hi_ready = sem("hi_ready")
        lo_ready = sem("lo_ready")
        panel_used = sem("panel_used")
        x_loaded = sem("x_loaded")
        gains_loaded = sem("gains_loaded")
        late_loaded = sem("late_loaded")
        consts = sem("consts")
        const_step = sem("const_step")
        gains_turned = sem("gains_turned")
        gains_ready = sem("gains_ready")
        act_step = sem("act_step")
        dve_step = sem("dve_step")
        sq_done = sem("sq_done")
        ms_ready = sem("ms_ready")
        std_ready = sem("std_ready")
        xn_ready = sem("xn_ready")
        tr_done = sem("tr_done")
        hi_done = sem("hi_done")
        lo_done = sem("lo_done")
        group_free = [sem("group_free0"), sem("group_free1")]
        act_read = sem("act_read")
        sig_ready = sem("sig_ready")
        ln_ready = sem("ln_ready")
        arg_ready = sem("arg_ready")
        e1_ready = sem("e1_ready")
        e2_ready = sem("e2_ready")
        alpha_ready = sem("alpha_ready")
        alpha_arg = sem("alpha_arg")
        qk_ready = sem("qk_ready")
        v_ready = sem("v_ready")
        g_ready = sem("g_ready")
        kt_done = sem("kt_done")
        kt_evac = sem("kt_evac")
        a_done = sem("a_done")
        at_evac = sem("at_evac")
        u_done = sem("u_done")
        u_free = sem("u_free")
        s_ready = sem("s_ready")
        o_done = sem("o_done")
        o_evac = sem("o_evac")
        o_sq = sem("o_sq")
        o_ms = sem("o_ms")
        o_std = sem("o_std")
        on_ready = sem("on_ready")
        ot_done = sem("ot_done")
        ot_hi = sem("ot_hi")
        ot_lo = sem("ot_lo")
        x_added = sem("x_added")
        silu_ready = sem("silu_ready")
        ahi_ready = sem("ahi_ready")
        alo_ready = sem("alo_ready")
        sc_done = sem("sc_done")
        sc_read = sem("sc_read")
        max_ready = sem("max_ready")
        exp_ready = sem("exp_ready")
        p_ready = sem("p_ready")
        pt_done = sem("pt_done")
        pt_evac = sem("pt_evac")
        ov_done = sem("ov_done")
        ov_hi = sem("ov_hi")
        ov_lo = sem("ov_lo")
        h_ready = sem("h_ready")
        hf_ready = sem("hf_ready")
        logits_done = sem("logits_done")
        gap_ready = sem("gap_ready")
        gate_exp = sem("gate_exp")
        picked = sem("picked")
        ranks_done = sem("ranks_done")
        info_ready = sem("info_ready")
        m_silu = sem("m_silu")
        m_act = sem("m_act")
        m_turn = sem("m_turn")
        m_ahi = sem("m_ahi")
        m_alo = sem("m_alo")
        m_out = sem("m_out")
        m_scat = sem("m_scat")
        m_add = sem("m_add")
        m_selturn = sem("m_selturn")
        m_selT = sem("m_selT")
        m_sel = sem("m_sel")
        m_gath = sem("m_gath")
        m_ghi = sem("m_ghi")
        m_glo = sem("m_glo")
        out_ready = sem("out_ready")
        out_stored = sem("out_stored")

        block = ctx.enter_context(nc.Block())

        def heads(t):
            return t[:].rearrange("p (h s) -> p h s", h=H)

        def tokens(t):
            return t[:].rearrange("p (t d) -> p t d", t=TT)

        def chunks(t):
            return t[:].rearrange("p (n c) -> p n c", c=CH)

        def pair(g):
            return 4 + 2 * (g % 2)

        def landed(eng, c, passes=0):
            eng.wait_ge(raw_landed[c % RAW_SLOTS], passes * (32 * (NP // RAW_SLOTS)) + 32 * (c // RAW_SLOTS + 1))

        def split_hi(act, c, passes=0):
            landed(act, c, passes)
            if c >= SPLIT_SLOTS:
                act.wait_ge(panel_used, passes * NP + c - SPLIT_SLOTS + 1)
            nc.scalar.activation(w_hi[:, c % SPLIT_SLOTS, :], w_raw[:, c % RAW_SLOTS, :], ACT.Copy).then_inc(hi_ready, 1)

        def split_lo(dve, c, passes=0):
            dve.wait_ge(hi_ready, passes * NP + c + 1)
            nc.vector.tensor_tensor(w_lo[:, c % SPLIT_SLOTS, :], w_raw[:, c % RAW_SLOTS, :],
                                    w_hi[:, c % SPLIT_SLOTS, :].bitcast(F32), ALU.subtract).then_inc(lo_ready, 1)

        def moe_gu(e, j, m):
            v = moe_w_gu[0, e].rearrange("(k p) (u f) -> p k u f", p=P, u=2)
            return [("u", v[:, 2 * m:2 * m + 2, u, j * 512:(j + 1) * 512]) for u in range(2)]

        def moe_down(e, j, m):
            v = moe_w_down[0, e].rearrange("(k p) c -> p k c", p=P)
            return halves(v[:, 4 * j + 2 * m:4 * j + 2 * m + 2, :])

        @block.sync
        def _(sp):
            def load(c, src, passes=0):
                if c >= RAW_SLOTS:
                    sp.wait_ge(lo_ready, passes * NP + c - RAW_SLOTS + 1)
                for n, (cut, part) in enumerate(src):
                    k = part.shape[1]
                    if cut == "k":
                        dst = w_raw[:, c % RAW_SLOTS, :].rearrange("p (n k f) -> p n k f", n=2, k=k)[:, n]
                    else:
                        dst = w_raw[:, c % RAW_SLOTS, :].rearrange("p (k u f) -> p k u f", k=k, u=2)[:, :, n]
                    sp.dma_start(dst, part).then_inc(raw_landed[c % RAW_SLOTS], 16)

            for c, src in enumerate(dense):
                load(c, src)

            def expert(e, passes):
                for c, (kind, j, m) in enumerate(moe_panels):
                    load(MOE0 + c, moe_gu(e, j, m) if kind == "G" else moe_down(e, j, m), passes)

            with sp.Fori(0, E) as e:
                expert(e, e)
            sp.wait_ge(info_ready, 1)
            extra = sp.value_load(info[0:1, 0:1], min_val=0, max_val=EXTRA)
            with sp.If(extra > 0):
                with sp.Fori(0, extra) as i:
                    e = sp.value_load(info[0:1, bass.ds(i + 1, 1)], min_val=0, max_val=E - 1)
                    expert(e, i + E)
            for c in range(SPLIT_SLOTS):
                kind, j, m = moe_panels[c]
                load(MOE0 + c, moe_gu(0, j, m), extra + E)
            for c in range(SPLIT_SLOTS):
                landed(sp, MOE0 + c, extra + E)
            sp.wait_ge(out_ready, 2)
            sp.dma_start(out.rearrange("b (t p) d -> p (b t) d", p=P), tokens(xn)).then_inc(out_stored, 16)
            sp.wait_ge(out_stored, 16)

        @block.gpsimd
        def _(pool):
            pool.dma_start(x_res[:], x.rearrange("b (t p) d -> p (b t) d", p=P)).then_inc(x_loaded, 16)
            for n, (src, lines) in enumerate(((attn_norm, 2 * KT), (ffn_norm, 2 * KT), (hgrn_out_norm, KT))):
                at = (0, 2 * KT, 4 * KT)[n]
                pool.dma_start(gain_rows[at:at + lines, :], src.rearrange("l (k p) -> (l k) p", p=P)).then_inc(gains_loaded, 16)
            pool.dma_start(gain_rows[5 * KT:6 * KT, :], kv_norm.rearrange("(k p) -> k p", p=P)).then_inc(gains_loaded, 16)
            nc.gpsimd.memset(ident[:], 0.0).then_inc(const_step, 1)
            nc.gpsimd.memset(chunk_mask[:], 1.0).then_inc(const_step, 1)
            nc.gpsimd.memset(earlier[:], 1.0).then_inc(const_step, 1)
            nc.gpsimd.memset(scan_keep[:], 1.0).then_inc(const_step, 1)
            nc.gpsimd.iota(alibi[:, 0:P], [[1, P]], base=0, channel_multiplier=-1,
                           allow_small_or_imprecise_dtypes=True).then_inc(const_step, 1)
            nc.gpsimd.iota(alibi[:, P:3 * P], [[1, 2 * P]], base=-P, channel_multiplier=-1,
                           allow_small_or_imprecise_dtypes=True).then_inc(const_step, 1)
            nc.gpsimd.iota(slot_id[:], [[1, P]], base=0, channel_multiplier=0,
                           allow_small_or_imprecise_dtypes=True).then_inc(consts, 1)
            nc.gpsimd.iota(expert_id[:], [[1, E]], base=0, channel_multiplier=0,
                           allow_small_or_imprecise_dtypes=True).then_inc(consts, 1)
            nc.gpsimd.memset(ones[:], 1.0).then_inc(consts, 1)
            pool.wait_ge(const_step, 6)
            nc.gpsimd.affine_select(ident[:], ident[:], [[-1, P]], ALU.not_equal, 1.0, base=0,
                                    channel_multiplier=1).then_inc(consts, 1)
            nc.gpsimd.affine_select(chunk_mask[:], chunk_mask[:], [[1, P]], ALU.is_ge, 0.0, base=0,
                                    channel_multiplier=-1).then_inc(const_step, 1)
            nc.gpsimd.affine_select(earlier[:], earlier[:], [[1, P]], ALU.is_gt, 0.0, base=0,
                                    channel_multiplier=-1).then_inc(consts, 1)
            nc.gpsimd.memset(scan_keep[:, :, 0:1], 0.0).then_inc(consts, 1)
            nc.gpsimd.affine_select(alibi[:, 0:P], alibi[:, 0:P], [[-1, P]], ALU.is_ge, -1e30, base=0,
                                    channel_multiplier=1).then_inc(consts, 1)
            nc.gpsimd.affine_select(alibi[:, P:3 * P], alibi[:, P:3 * P], [[-1, 2 * P]], ALU.is_ge, -1e30, base=P,
                                    channel_multiplier=1).then_inc(consts, 1)
            pool.wait_ge(const_step, 7)
            nc.gpsimd.memset(chunk_mask[0:CH, CH:P], 0.0).then_inc(consts, 1)
            pool.dma_start(router[:], moe_router[0].rearrange("(k p) e -> p k e", p=P)).then_inc(late_loaded, 16)
            pool.wait_ge(ot_done, 4)
            pool.dma_start(work[7][:, 0:D], ffn_norm[1].partition_broadcast(P)).then_inc(late_loaded, 16)
            pool.dma_start(work[7][:, D:2 * D], final_norm.partition_broadcast(P)).then_inc(late_loaded, 16)
            pool.wait_ge(late_loaded, 48)

        CONSTS = 9

        @block.scalar
        def _(act):
            steps = [0]

            def link(ins):
                steps[0] += 1
                ins.then_inc(act_step, 1)
                act.wait_ge(act_step, steps[0])

            def norm_stats(n):
                for t in range(TT):
                    nc.scalar.activation(junk[:], x_res[:, t, :], ACT.Square,
                                         accum_out=sumsq[:, n, t:t + 1]).then_inc(sq_done, 1)
                    act.wait_ge(sq_done, TT * n + t + 1)
                act.wait_ge(ms_ready, n + 1)
                nc.scalar.activation(std[:, n, :], mean_sq[:, n, :], ACT.Sqrt).then_inc(std_ready, 1)

            def norm_hi(gain, tr, hi):
                for b in range(4):
                    act.wait_ge(tr_done, tr + b + 1)
                    for i in range(2):
                        ins = nc.scalar.activation(h_hi[:, 2 * b + i, :], ps[:, b, i * S:(i + 1) * S], ACT.Copy,
                                                   scale=gains[:, gain + 2 * b + i:gain + 2 * b + i + 1])
                    ins.then_inc(hi_done, 1)

            act.wait_ge(gains_turned, 1)
            nc.scalar.activation(gains[:], ps[:, 4, 0:6 * KT], ACT.Copy).then_inc(gains_ready, 1)
            act.wait_ge(gains_ready, 1)
            act.wait_ge(x_loaded, 16)
            norm_stats(0)
            for c in range(SPLIT_SLOTS):
                split_hi(act, c)
            norm_hi(GAIN_ATTN0, 0, 0)

            for c in range(AT_WO):
                split_hi(act, c + SPLIT_SLOTS)
                g = c // 2
                b = pair(g)
                both = ps[:, b:b + 2, :].rearrange("p b f -> p (b f)")
                half = slice(1024 * (g % 2), 1024 * (g % 2) + 1024)
                if c % 2 == 1:
                    act.wait_ge(panel_used, c + 1)
                    if g < 2:
                        nc.scalar.activation(kT[:, half], both, ACT.Sigmoid, scale=-1.0)
                        nc.scalar.activation(tT[:, half], both, ACT.Abs).then_inc(act_read, 1)
                    elif g < 4:
                        nc.scalar.activation(qT[:, half], both, ACT.Sigmoid).then_inc(act_read, 1)
                    elif g < 6:
                        for t in range(TT):
                            ins = nc.scalar.activation(tokens(v_tm)[:, t, 512 * (g % 2):512 * (g % 2) + 512],
                                                       ps[:, b + t, :], ACT.Copy)
                        ins.then_inc(group_free[g % 2], 1)
                    else:
                        for t in range(TT):
                            ins = nc.scalar.activation(tokens(g_tm)[:, t, 512 * (g % 2):512 * (g % 2) + 512],
                                                       ps[:, b + t, :], ACT.Sigmoid)
                        ins.then_inc(act_read, 1)
                if c == 3:
                    act.wait_ge(act_read, 2)
                    nc.scalar.activation(tT[:], tT[:], ACT.Sigmoid).then_inc(sig_ready, 1)
                if c == 7:
                    act.wait_ge(sig_ready, 1)
                    nc.scalar.activation(tT[:], tT[:], ACT.Ln).then_inc(ln_ready, 1)
                if c == 11:
                    act.wait_ge(arg_ready, 1)
                    nc.scalar.activation(tT[:], zT[:], ACT.Exp).then_inc(e1_ready, 1)
                    act.wait_ge(e1_ready, 1)
                    nc.scalar.activation(zT[:], zT[:], ACT.Exp, scale=-1.0).then_inc(e2_ready, 1)
                    nc.scalar.activation(alpha[:], alpha[:], ACT.Exp).then_inc(alpha_ready, 1)

            for t in range(TT):
                for b in range(2):
                    act.wait_ge(kt_done, 2 * t + b + 1)
                    act.wait_ge(qk_ready, 2)
                    nc.scalar.activation(tokens(zT)[:, t, b * 512:(b + 1) * 512], ps[:, b, :], ACT.Copy).then_inc(kt_evac, 1)
            for t in range(TT):
                act.wait_ge(o_done, t + 1)
                both = ps[:, 6:8, :].rearrange("p b f -> p (b f)")
                nc.scalar.activation(tokens(kT)[:, t, :], both, ACT.Copy).then_inc(o_evac, 1)
                if t:
                    act.wait_ge(o_ms, t)
                nc.scalar.activation(junk[:], both, ACT.Square).then_inc(o_sq, 1)
                act.wait_ge(o_ms, t + 1)
                nc.scalar.activation(head_std[:, t, :], head_ms[:, t, :], ACT.Sqrt).then_inc(o_std, 1)
            for t in range(TT):
                for b in range(2):
                    act.wait_ge(ot_done, 2 * t + b + 1)
                    for i in range(4):
                        k = 4 * b + i
                        ins = nc.scalar.activation(h_hi[:, k, t * P:(t + 1) * P], ps[:, b, i * P:(i + 1) * P], ACT.Copy,
                                                   scale=gains[:, GAIN_OUT + k:GAIN_OUT + k + 1])
                    ins.then_inc(ot_hi, 1)
            for c in range(AT_WO, AT_FFN):
                split_hi(act, c + SPLIT_SLOTS)

            act.wait_ge(group_free[1], (GR_WO + 1) // 2 + 1)
            norm_stats(1)
            norm_hi(GAIN_FFN0, 4, 4)
            for n, (kind, j, m) in enumerate(ffn_panels):
                split_hi(act, AT_FFN + n + SPLIT_SLOTS)
                if kind == "G" and m == 1:
                    g = GR_FFN + j
                    b = pair(g)
                    act.wait_ge(panel_used, AT_FFN + n + 1)
                    if j >= 2:
                        act.wait_ge(alo_ready, j - 1)
                    s = junk[:, 512 * (j % 2):512 * (j % 2) + 512]
                    nc.scalar.activation(s.rearrange("p (b f) -> p b f", b=2), ps[:, b:b + 2, 0:S], ACT.Silu).then_inc(silu_ready, 1)
                    act.wait_ge(group_free[g % 2], g // 2 + 1)
                    if j >= 2:
                        act.wait_ge(panel_used, AT_FFN + ffn_end["D", j - 2])
                    nc.scalar.activation(a_hi[:, j % 2, :], s, ACT.Copy).then_inc(ahi_ready, 1)

            act.wait_ge(x_added, 4)
            norm_stats(2)
            norm_hi(GAIN_ATTN1, 8, 8)
            for c in range(AT_Q, AT_WO2):
                split_hi(act, c + SPLIT_SLOTS)
                g = GR_Q + (c - AT_Q) // 2
                b = pair(g)
                if (c - AT_Q) % 2 == 1:
                    act.wait_ge(panel_used, c + 1)
                    n = (g - GR_Q) // 2
                    i = (g - GR_Q) % 2
                    if n < 2:
                        nc.scalar.activation((qT, kT)[n][:, 1024 * i:1024 * i + 1024],
                                             ps[:, b:b + 2, :].rearrange("p b f -> p (b f)"), ACT.Copy).then_inc(group_free[g % 2], 1)
                    else:
                        for t in range(TT):
                            ins = nc.scalar.activation(tokens(v_tm)[:, t, 512 * i:512 * i + 512], ps[:, b + t, :], ACT.Copy)
                        ins.then_inc(group_free[g % 2], 1)
                if c == AT_KV - 1:
                    norm_hi(GAIN_KV, 8, 12)

            def probabilities(h):
                act.wait_ge(max_ready, h + 1)
                p = work[5][:, 512 * (h % 2):512 * (h % 2) + 384]
                for t in range(TT):
                    part = p[:, 0:P] if t == 0 else p[:, P:3 * P]
                    ins = nc.scalar.activation(part, part, ACT.Exp, bias=soft[:, h, 2 + t:3 + t], scale=SCALE,
                                               accum_out=soft[:, h, 4 + t:5 + t])
                ins.then_inc(exp_ready, 1)

            def attended_hi(h):
                act.wait_ge(ov_done, h + 1)
                nc.scalar.activation(h_hi[:, h, :], ps[:, 4 + h % 2, 0:S], ACT.Copy).then_inc(ov_hi, 1)

            probabilities(0)
            for h in range(H):
                if h + 1 < H:
                    probabilities(h + 1)
                act.wait_ge(pt_done, h + 1)
                if h >= 2:
                    act.wait_ge(ov_done, h - 1)
                nc.scalar.activation(work[5][:, 1024 + 512 * (h % 2):1024 + 512 * (h % 2) + 384],
                                     ps[:, 2 + h % 2, 0:384], ACT.Copy).then_inc(pt_evac, 1)
                if h:
                    attended_hi(h - 1)
            attended_hi(H - 1)
            for c in range(AT_WO2, MOE0):
                split_hi(act, c + SPLIT_SLOTS)

            act.wait_ge(group_free[(GR_WO2 + 1) % 2], (GR_WO2 + 1) // 2 + 1)
            norm_stats(3)
            for b in range(4):
                act.wait_ge(tr_done, 12 + b + 1)
                nc.scalar.activation(qT[:, 512 * b:512 * b + 512], ps[:, b, :], ACT.Copy).then_inc(hf_ready, 1)
            act.wait_ge(gap_ready, 1)
            nc.scalar.activation(route[:, :, 3, 0:1], route[:, :, 2, 0:1], ACT.Exp).then_inc(gate_exp, 1)

            def gather_hi(passes):
                for b in range(2):
                    act.wait_ge(m_gath, 2 * passes + b + 1)
                    nc.scalar.activation(h_hi[:, 4 * b:4 * b + 4, 0:P],
                                         ps[:, (7, 2)[b], :].rearrange("p (k s) -> p k s", k=4), ACT.Copy).then_inc(m_ghi, 1)

            gather_hi(0)

            def expert(p):
                def turned_hi(j):
                    act.wait_ge(m_turn, p * EG + j + 1)
                    act.wait_ge(panel_used, p * NP + MOE0 + (moe_end["D", j - 2] if j >= 2 else 0))
                    nc.scalar.activation(a_hi[:, j % 2, :], ps[:, 6, :], ACT.Copy).then_inc(m_ahi, 1)

                for c, (kind, j, m) in enumerate(moe_panels):
                    split_hi(act, MOE0 + c + SPLIT_SLOTS, p)
                    if kind == "G" and m == 1 and j >= 1:
                        turned_hi(j - 1)
                    if kind == "G" and m == 3:
                        act.wait_ge(panel_used, p * NP + MOE0 + c + 1)
                        if j >= 2:
                            act.wait_ge(m_turn, p * EG + j - 1)
                        nc.scalar.activation(junk[:, 512 * (j % 2):512 * (j % 2) + 512], ps[:, 2 * (j % 2), :],
                                             ACT.Silu).then_inc(m_silu, 1)
                        if j == 2:
                            act.wait_ge(m_selturn, p + 1)
                            nc.scalar.activation(sel_T[:], ps[:, 7, 0:S], ACT.Copy).then_inc(m_selT, 1)
                    if kind == "D" and j == EG - 2 and m == 1:
                        turned_hi(EG - 1)
                        gather_hi(p + 1)
                act.wait_ge(panel_used, p * NP + MOE0 + NP)
                nc.scalar.activation(work[1][:, 0:D], ps[:, 4:6, :].rearrange("p b f -> p (b f)"), ACT.Copy).then_inc(m_out, 1)

            with act.Fori(0, E) as p:
                expert(p)
            act.wait_ge(info_ready, 1)
            extra = act.value_load(info[0:1, 0:1], min_val=0, max_val=EXTRA)
            with act.If(extra > 0):
                with act.Fori(0, extra) as i:
                    expert(i + E)
            act.wait_ge(m_add, (extra + E) * 4 + 4)
            norm_stats(4)

        @block.vector
        def _(dve):
            steps = [0]

            def link(ins):
                steps[0] += 1
                ins.then_inc(dve_step, 1)
                dve.wait_ge(dve_step, steps[0])

            def norm_scale(n):
                dve.wait_ge(sq_done, TT * n + TT)
                nc.vector.tensor_scalar(mean_sq[:, n, :], sumsq[:, n, :], 1.0 / D, EPS, ALU.mult, ALU.add).then_inc(ms_ready, 1)
                dve.wait_ge(std_ready, n + 1)
                link(nc.vector.reciprocal(rstd[:, n, :], std[:, n, :]))

            def norm_tokens(n):
                for t in range(TT):
                    nc.vector.tensor_scalar(tokens(xn)[:, t, :], x_res[:, t, :], rstd[:, n, t:t + 1], None,
                                            ALU.mult).then_inc(xn_ready, 1)

            def norm_lo(gain, hi):
                for b in range(4):
                    dve.wait_ge(hi_done, hi + b + 1)
                    for i in range(2):
                        k = 2 * b + i
                        ins = nc.vector.scalar_tensor_tensor(h_lo[:, k, :], ps[:, b, i * S:(i + 1) * S],
                                                             gains[:, gain + k:gain + k + 1], h_hi[:, k, :].bitcast(F32),
                                                             ALU.mult, ALU.subtract)
                    ins.then_inc(lo_done, 1)

            def add_group(c, g, i):
                dve.wait_ge(panel_used, c + 1)
                for t in range(TT):
                    xs = x_res[:, t, 512 * i:512 * i + 512]
                    ins = nc.vector.tensor_tensor(xs, xs, ps[:, pair(g) + t, :], ALU.add)
                ins.then_inc(group_free[g % 2], 1)

            norm_scale(0)
            norm_tokens(0)
            for c in range(SPLIT_SLOTS):
                split_lo(dve, c)
            dve.wait_ge(gains_ready, 1)
            norm_lo(GAIN_ATTN0, 0)

            dve.wait_ge(consts, CONSTS)
            for c in range(AT_WO):
                split_lo(dve, c + SPLIT_SLOTS)
                g = c // 2
                b = pair(g)
                both = ps[:, b:b + 2, :].rearrange("p b f -> p (b f)")
                half = slice(1024 * (g % 2), 1024 * (g % 2) + 1024)
                if c % 2 == 1:
                    if g < 2:
                        dve.wait_ge(act_read, g + 1)
                        nc.vector.tensor_scalar(zT[:, half], both, 0.0, None, ALU.min).then_inc(group_free[g % 2], 1)
                    elif g < 4:
                        dve.wait_ge(act_read, g + 1)
                        nc.vector.tensor_tensor(qT[:, half], qT[:, half], both, ALU.mult).then_inc(group_free[g % 2], 1)
                    elif g >= 6:
                        dve.wait_ge(act_read, g - 1)
                        for t in range(TT):
                            gs = tokens(g_tm)[:, t, 512 * (g % 2):512 * (g % 2) + 512]
                            ins = nc.vector.tensor_tensor(gs, gs, ps[:, b + t, :], ALU.mult)
                        ins.then_inc(group_free[g % 2], 1)
                if c == 8:
                    dve.wait_ge(ln_ready, 1)
                    dve.wait_ge(group_free[1], 1)
                    link(nc.vector.tensor_tensor(zT[:], zT[:], tT[:], ALU.add))
                if c in (8, 9):
                    for h in range(4 * (c - 8), 4 * (c - 8) + 4):
                        ins = nc.vector.tensor_tensor_scan(heads(tT)[:, h, :], scan_keep[:].rearrange("p n c -> p (n c)"),
                                                           heads(zT)[:, h, :], 0.0, ALU.mult, ALU.add)
                if c == 9:
                    link(ins)
                    by_chunk = heads(tT).rearrange("p h (n c) -> p h n c", c=CH)
                    nc.vector.tensor_copy(b_ref[:], by_chunk[:, :, :, CH // 2 - 1])
                    link(nc.vector.tensor_copy(b_last[:], by_chunk[:, :, :, CH - 1]))
                    link(nc.vector.tensor_tensor(alpha[:, :, 0:NCH - 1], b_ref[:, :, 1:NCH], b_ref[:, :, 0:NCH - 1], ALU.subtract))
                    nc.vector.tensor_tensor(alpha[:, :, 0:NCH - 1], alpha[:, :, 0:NCH - 1], b_last[:, :, 0:NCH - 1], ALU.add)
                    nc.vector.memset(alpha[:, :, NCH - 1:NCH], 0.0)
                    ref = b_ref[:].rearrange("p h n -> p (h n)").unsqueeze(2).broadcast_to([P, H * NCH, CH])
                    nc.vector.tensor_tensor(chunks(zT), chunks(tT), ref, ALU.subtract).then_inc(arg_ready, 1)
                if c == 12:
                    dve.wait_ge(e1_ready, 1)
                    dve.wait_ge(group_free[1], 2)
                    nc.vector.tensor_tensor(qT[:], qT[:], tT[:], ALU.mult).then_inc(qk_ready, 1)
                if c == 13:
                    dve.wait_ge(e2_ready, 1)
                    nc.vector.tensor_tensor(kT[:], kT[:], zT[:], ALU.mult).then_inc(qk_ready, 1)

            states = [work[6][:, 0:D], work[6][:, D:2 * D], work[7][:, 0:D]]
            summed = work[7][:, D:2 * D]
            dve.wait_ge(alpha_ready, 1)
            dve.wait_ge(qk_ready, 1)
            link(nc.vector.memset(tT[:], 0.0))

            def keep_causal(t):
                dve.wait_ge(a_done, t + 1)
                for h in range(H):
                    ins = nc.vector.copy_predicated(tokens(tT)[:, t, h * P:(h + 1) * P], chunk_mask[:].bitcast(U32),
                                                    ps[:, 4 + h // 4, (h % 4) * P:(h % 4) * P + P])
                ins.then_inc(at_evac, 1)

            def by_head(a):
                return a.rearrange("p (h v) -> p h v", h=H)

            def carry(n):
                return alpha[:, :, n:n + 1].broadcast_to([P, H, P])

            u_sums = ps[:, 2:4, :].rearrange("p b (h v) -> p (b h) v", v=P)
            keep_causal(0)
            dve.wait_ge(u_done, 1)
            nc.vector.tensor_tensor(by_head(states[0]), u_sums, carry(0), ALU.mult).then_inc(s_ready, 1)
            keep_causal(1)
            for n in (1, 2):
                dve.wait_ge(s_ready, n)
                dve.wait_ge(u_done, n + 1)
                nc.vector.tensor_tensor(by_head(summed), by_head(states[n - 1]), u_sums, ALU.add).then_inc(u_free, 1)
                dve.wait_ge(u_free, n)
                nc.vector.tensor_tensor(by_head(states[n]), by_head(summed), carry(n), ALU.mult).then_inc(s_ready, 1)
            for t in range(TT):
                dve.wait_ge(o_sq, t + 1)
                link(nc.vector.tensor_reduce(head_rstd[:, t, :], by_head(junk[:]), AX_X, ALU.add))
                nc.vector.tensor_scalar(head_ms[:, t, :], head_rstd[:, t, :], 1.0 / P, EPS, ALU.mult, ALU.add).then_inc(o_ms, 1)
                dve.wait_ge(o_std, t + 1)
                link(nc.vector.reciprocal(head_rstd[:, t, :], head_std[:, t, :]))
                o = tokens(kT)[:, t, :]
                link(nc.vector.tensor_tensor(by_head(o), by_head(o), head_rstd[:, t, :].unsqueeze(2).broadcast_to([P, H, P]), ALU.mult))
                nc.vector.tensor_tensor(o, o, tokens(g_tm)[:, t, :], ALU.mult).then_inc(on_ready, 1)
            for t in range(TT):
                for b in range(2):
                    dve.wait_ge(ot_hi, 2 * t + b + 1)
                    for i in range(4):
                        k = 4 * b + i
                        ins = nc.vector.scalar_tensor_tensor(h_lo[:, k, t * P:(t + 1) * P], ps[:, b, i * P:(i + 1) * P],
                                                             gains[:, GAIN_OUT + k:GAIN_OUT + k + 1],
                                                             h_hi[:, k, t * P:(t + 1) * P].bitcast(F32), ALU.mult, ALU.subtract)
                    ins.then_inc(ot_lo, 1)
            for c in range(AT_WO, AT_FFN):
                split_lo(dve, c + SPLIT_SLOTS)
                if (c - AT_WO) % 2 == 1:
                    i = (c - AT_WO) // 2
                    add_group(c, GR_WO + i, i)

            dve.wait_ge(group_free[1], (GR_WO + 1) // 2 + 1)
            norm_scale(1)
            norm_tokens(1)
            norm_lo(GAIN_FFN0, 4)
            for n, (kind, j, m) in enumerate(ffn_panels):
                split_lo(dve, AT_FFN + n + SPLIT_SLOTS)
                if kind == "G" and m == 1:
                    g = GR_FFN + j
                    b = pair(g)
                    s = junk[:, 512 * (j % 2):512 * (j % 2) + 512]
                    s2 = s.rearrange("p (b f) -> p b f", b=2)
                    dve.wait_ge(silu_ready, j + 1)
                    nc.vector.tensor_tensor(s2, s2, ps[:, b:b + 2, S:2 * S], ALU.mult).then_inc(group_free[g % 2], 1)
                    dve.wait_ge(ahi_ready, j + 1)
                    nc.vector.tensor_tensor(a_lo[:, j % 2, :], s, a_hi[:, j % 2, :].bitcast(F32), ALU.subtract).then_inc(alo_ready, 1)
            dve.wait_ge(panel_used, AT_Q)
            for t in range(TT):
                for i in range(2):
                    xs = x_res[:, t, 512 * i:512 * i + 512]
                    nc.vector.tensor_tensor(xs, xs, ps[:, 2 * t + i, :], ALU.add).then_inc(x_added, 1)

            dve.wait_ge(x_added, 4)
            norm_scale(2)
            norm_tokens(2)
            norm_lo(GAIN_ATTN1, 8)
            for c in range(AT_Q, AT_WO2):
                split_lo(dve, c + SPLIT_SLOTS)
                if c == AT_KV - 1:
                    norm_lo(GAIN_KV, 12)

            def biased(h):
                p = work[5][:, 512 * (h % 2):512 * (h % 2) + 384]
                dve.wait_ge(sc_done, h + 1)
                if h >= 2:
                    dve.wait_ge(pt_done, h - 1)
                nc.vector.scalar_tensor_tensor(p, alibi[:], SLOPES[h] / SCALE, ps[:, h % 2, 0:384],
                                               ALU.mult, ALU.add).then_inc(sc_read, 1)
                dve.wait_ge(sc_read, h + 1)
                nc.vector.tensor_reduce(soft[:, h, 0:1], p[:, 0:P], AX_X, ALU.max)
                link(nc.vector.tensor_reduce(soft[:, h, 1:2], p[:, P:3 * P], AX_X, ALU.max))
                nc.vector.tensor_scalar(soft[:, h, 2:4], soft[:, h, 0:2], -SCALE, None, ALU.mult).then_inc(max_ready, 1)

            def attended_lo(h):
                dve.wait_ge(ov_hi, h + 1)
                nc.vector.tensor_tensor(h_lo[:, h, :], ps[:, 4 + h % 2, 0:S], h_hi[:, h, :].bitcast(F32),
                                        ALU.subtract).then_inc(ov_lo, 1)

            biased(0)
            for h in range(H):
                if h + 1 < H:
                    biased(h + 1)
                p = work[5][:, 512 * (h % 2):512 * (h % 2) + 384]
                dve.wait_ge(exp_ready, h + 1)
                link(nc.vector.reciprocal(soft[:, h, 6:8], soft[:, h, 4:6]))
                nc.vector.tensor_scalar(p[:, 0:P], p[:, 0:P], soft[:, h, 6:7], None, ALU.mult)
                nc.vector.tensor_scalar(p[:, P:3 * P], p[:, P:3 * P], soft[:, h, 7:8], None, ALU.mult).then_inc(p_ready, 1)
                if h:
                    attended_lo(h - 1)
            attended_lo(H - 1)
            for c in range(AT_WO2, MOE0):
                split_lo(dve, c + SPLIT_SLOTS)
                if (c - AT_WO2) % 2 == 1:
                    i = (c - AT_WO2) // 2
                    add_group(c, GR_WO2 + i, i)

            dve.wait_ge(group_free[(GR_WO2 + 1) % 2], (GR_WO2 + 1) // 2 + 1)
            norm_scale(3)
            norm_tokens(3)
            dve.wait_ge(xn_ready, 8)
            dve.wait_ge(late_loaded, 48)
            for t in range(TT):
                ht = tokens(xn)[:, t, :]
                nc.vector.tensor_tensor(ht, ht, work[7][:, 0:D], ALU.mult).then_inc(h_ready, 1)

            r = route
            dve.wait_ge(logits_done, 1)
            link(nc.vector.tensor_copy(r[:, :, 0, :], ps[:, 4, 0:TT * E].rearrange("p (t e) -> p t e", t=TT)))
            for t in range(TT):
                ins = nc.vector.max(r[:, t, 1, :], r[:, t, 0, :])
            link(ins)
            for t in range(TT):
                ins = nc.vector.max_index(route_u[:, t, :], r[:, t, 1, :], r[:, t, 0, :])
            link(ins)
            nc.vector.tensor_tensor(r[:, :, 2, 0:1], r[:, :, 1, 1:2], r[:, :, 1, 0:1], ALU.subtract).then_inc(gap_ready, 1)
            link(nc.vector.tensor_copy(r[:, :, 4, :], route_u[:]))
            for t in range(TT):
                for i in range(2):
                    ins = nc.vector.tensor_scalar(r[:, t, 5 + i, :], expert_id[:], r[:, t, 4, i:i + 1], None, ALU.is_equal)
            link(ins)
            nc.vector.tensor_tensor(r[:, :, 7, :], r[:, :, 5, :], r[:, :, 6, :], ALU.add).then_inc(picked, 1)
            dve.wait_ge(gate_exp, 1)
            link(nc.vector.tensor_scalar(r[:, :, 2, 1:2], r[:, :, 3, 0:1], 1.0, None, ALU.add))
            link(nc.vector.reciprocal(r[:, :, 2, 2:3], r[:, :, 2, 1:2]))
            link(nc.vector.tensor_tensor(r[:, :, 2, 3:4], r[:, :, 2, 2:3], r[:, :, 3, 0:1], ALU.mult))
            for t in range(TT):
                link(nc.vector.tensor_scalar(r[:, t, 8, :], r[:, t, 6, :], r[:, t, 2, 3:4], None, ALU.mult))
                ins = nc.vector.scalar_tensor_tensor(r[:, t, 9, :], r[:, t, 5, :], r[:, t, 2, 2:3], r[:, t, 8, :], ALU.mult, ALU.add)
            link(ins)
            dve.wait_ge(ranks_done, 1)
            rank_ps = ps[:, 5, 0:TT * E].rearrange("p (t e) -> p t e", t=TT)
            link(nc.vector.scalar_tensor_tensor(r[:, :, 10, :], rank_ps, 1.0, r[:, :, 7, :], ALU.add, ALU.mult))
            link(nc.vector.tensor_scalar(r[:, :, 10, :], r[:, :, 10, :], -1.0, None, ALU.add))
            nc.vector.memset(pass_rank[:], -1.0)
            link(nc.vector.memset(pass_gate[:], 0.0))
            nc.vector.tensor_copy(pass_rank[:, :, 1:E + 1], r[:, :, 10, :])
            link(nc.vector.tensor_copy(pass_gate[:, :, 1:E + 1], r[:, :, 9, :]))
            for t in range(TT):
                ins = nc.vector.tensor_scalar(sel[:, t, :], slot_id[:], pass_rank[:, t, 1:2], None, ALU.is_equal)
            ins.then_inc(m_sel, 1)
            nc.vector.memset(sel_T[:], 0.0)
            nc.vector.memset(work[1][:, 0:D], 0.0).then_inc(m_out, 1)
            dve.wait_ge(m_sel, 1)
            nc.vector.tensor_scalar(over[:, 0, :], ps[:, 5, TT * E:TT * E + E], float(P), None, ALU.is_gt)
            link(nc.vector.memset(over[:, 7, :], 1.0))
            link(nc.vector.tensor_tensor_scan(over[:, 1, :], over[:, 7, :], over[:, 0, :], 0.0, ALU.mult, ALU.add))
            for k in range(EXTRA):
                link(nc.vector.tensor_scalar(over[:, 2, :], over[:, 1, :], float(k + 1), None, ALU.is_equal))
                link(nc.vector.tensor_tensor(over[:, 2, :], over[:, 2, :], over[:, 0, :], ALU.mult))
                link(nc.vector.tensor_tensor(over[:, 3, :], over[:, 2, :], expert_id[:], ALU.mult))
                link(nc.vector.tensor_reduce(info_f[:, k + 1:k + 2], over[:, 3, :], AX_X, ALU.add))
                for t in range(TT):
                    link(nc.vector.scalar_tensor_tensor(over[:, 4, :], r[:, t, 10, :], 1.0 - P, over[:, 2, :], ALU.add, ALU.mult))
                    link(nc.vector.tensor_reduce(over[:, 6, 0:1], over[:, 4, :], AX_X, ALU.add))
                    link(nc.vector.tensor_scalar(pass_rank[:, t, E + 1 + k:E + 2 + k], over[:, 6, 0:1], -1.0, None, ALU.add))
                    link(nc.vector.tensor_tensor(over[:, 5, :], r[:, t, 9, :], over[:, 2, :], ALU.mult))
                    link(nc.vector.tensor_reduce(pass_gate[:, t, E + 1 + k:E + 2 + k], over[:, 5, :], AX_X, ALU.add))
            link(nc.vector.tensor_copy(info_f[:, 0:1], over[:, 1, E - 1:E]))
            nc.vector.tensor_copy(info[:], info_f[:]).then_inc(info_ready, 1)
            dve.wait_ge(info_ready, 1)

            def gather_lo(passes):
                for b in range(2):
                    dve.wait_ge(m_ghi, 2 * passes + b + 1)
                    nc.vector.tensor_tensor(h_lo[:, 4 * b:4 * b + 4, 0:P], ps[:, (7, 2)[b], :].rearrange("p (k s) -> p k s", k=4),
                                            h_hi[:, 4 * b:4 * b + 4, 0:P].bitcast(F32), ALU.subtract).then_inc(m_glo, 1)

            gather_lo(0)

            def add_back(p, q):
                t, i = q // 2, q % 2
                dve.wait_ge(m_scat, p * 4 + q + 1)
                xs = x_res[:, t, 512 * i:512 * i + 512]
                nc.vector.scalar_tensor_tensor(xs, ps[:, 7, :], pass_gate[:, t, bass.ds(p, 1)], xs,
                                               ALU.mult, ALU.add).then_inc(m_add, 1)

            def expert(p):
                def turned_lo(j):
                    dve.wait_ge(m_ahi, p * EG + j + 1)
                    nc.vector.tensor_tensor(a_lo[:, j % 2, :], ps[:, 6, :], a_hi[:, j % 2, :].bitcast(F32),
                                            ALU.subtract).then_inc(m_alo, 1)

                for c, (kind, j, m) in enumerate(moe_panels):
                    split_lo(dve, MOE0 + c + SPLIT_SLOTS, p)
                    if kind == "G" and m == 1:
                        if j >= 1:
                            turned_lo(j - 1)
                        if j < 2:
                            add_back(p, 2 * j)
                    if kind == "G" and m == 3:
                        if j < 2:
                            add_back(p, 2 * j + 1)
                        dve.wait_ge(m_silu, p * EG + j + 1)
                        s = junk[:, 512 * (j % 2):512 * (j % 2) + 512]
                        nc.vector.tensor_tensor(s, s, ps[:, 2 * (j % 2) + 1, :], ALU.mult).then_inc(m_act, 1)
                        if j == 3:
                            dve.wait_ge(m_selturn, p + 1)
                            for t in range(TT):
                                ins = nc.vector.tensor_scalar(sel[:, t, :], slot_id[:], pass_rank[:, t, bass.ds(p + 2, 1)], None,
                                                              ALU.is_equal)
                            ins.then_inc(m_sel, 1)
                    if kind == "D" and j == EG - 2 and m == 1:
                        turned_lo(EG - 1)
                        gather_lo(p + 1)

            with dve.Fori(0, E) as p:
                expert(p)
            extra = dve.value_load(info[0:1, 0:1], min_val=0, max_val=EXTRA)
            with dve.If(extra > 0):
                with dve.Fori(0, extra) as i:
                    expert(i + E)
            for q in range(4):
                add_back(extra + E, q)
            norm_scale(4)
            for t in range(TT):
                ot = tokens(xn)[:, t, :]
                nc.vector.scalar_tensor_tensor(ot, x_res[:, t, :], rstd[:, 4, t:t + 1], work[7][:, D:2 * D],
                                               ALU.mult, ALU.mult).then_inc(out_ready, 1)

        @block.tensor
        def _(pe):
            def product(out_ap, lhs, rhs, start, stop, share=False):
                (lh, ll), (rh, rl) = lhs, rhs
                nc.tensor.matmul(out_ap, lh, rh, start=start, stop=False, skip_group_check=share)
                nc.tensor.matmul(out_ap, lh, rl, start=False, stop=False, skip_group_check=share)
                return nc.tensor.matmul(out_ap, ll, rh, start=False, stop=stop, skip_group_check=share)

            def weights(c, a, n):
                s = c % SPLIT_SLOTS
                return w_hi[:, s, a:a + n], w_lo[:, s, a:a + n]

            def acts(k, t0, n):
                return h_hi[:, k, t0:t0 + n], h_lo[:, k, t0:t0 + n]

            def feature_panel(c, g, kh):
                pe.wait_ge(lo_ready, c + 1)
                for k in range(4):
                    for f in range(4):
                        o = ps[:, pair(g) + f // 2, (f % 2) * S:(f % 2) * S + S]
                        ins = product(o, weights(c, k * 512 + f * P, P), acts(4 * kh + k, 0, S),
                                      start=(kh == 0 and k == 0 and f % 2 == 0), stop=(kh == 1 and k == 3), share=True)
                ins.then_inc(panel_used, 1)

            def token_panel(c, g, kh):
                pe.wait_ge(lo_ready, c + 1)
                for k in range(4):
                    for t in range(TT):
                        ins = product(ps[:, pair(g) + t, :], acts(4 * kh + k, t * P, P), weights(c, k * 512, 512),
                                      start=(kh == 0 and k == 0), stop=(kh == 1 and k == 3))
                ins.then_inc(panel_used, 1)

            def group_begins(g):
                if g >= 2:
                    pe.wait_ge(group_free[g % 2], g // 2)

            def turn_tokens(n, base):
                pe.wait_ge(xn_ready if n < 3 else h_ready, TT * (n + 1) if n < 3 else TT)
                for b in range(4):
                    for i in range(2):
                        for t in range(TT):
                            k = 2 * b + i
                            ins = nc.tensor.transpose(ps[:, b, i * S + t * P:i * S + (t + 1) * P],
                                                      tokens(xn)[:, t, k * P:(k + 1) * P], ident[:])
                    ins.then_inc(tr_done, 1)

            def run_group(c, g, panel, tiles=None):
                group_begins(g)
                for kh in range(2):
                    if tiles is not None:
                        pe.wait_ge(lo_done, tiles + 2 * kh + 2)
                    panel(c + kh, g, kh)

            pe.wait_ge(consts, CONSTS)
            pe.wait_ge(gains_loaded, 64)
            nc.tensor.transpose(ps[:, 4, 0:6 * KT], gain_rows[:], ident[0:6 * KT, 0:6 * KT]).then_inc(gains_turned, 1)
            turn_tokens(0, 0)
            pe.wait_ge(gains_ready, 1)
            for g in range(8):
                run_group(2 * g, g, feature_panel if g < 4 else token_panel, tiles=0 if g == 0 else None)

            def qh(h, a, n):
                return heads(qT)[:, h, a:a + n]

            def kh_(h, a, n):
                return heads(kT)[:, h, a:a + n]

            def vh(t, h, a=0, n=P):
                return tokens(v_tm)[a:a + n, t, h * P:(h + 1) * P]

            def turn_k(t):
                for b in range(2):
                    if t:
                        pe.wait_ge(kt_evac, b + 1)
                    for h in range(4 * b, 4 * b + 4):
                        ins = nc.tensor.transpose(ps[:, b, (h % 4) * P:(h % 4) * P + P], kh_(h, t * P, P), ident[:])
                    ins.then_inc(kt_done, 1)

            def scores(t):
                if t:
                    pe.wait_ge(at_evac, t)
                for h in range(H):
                    ins = nc.tensor.matmul(ps[:, 4 + h // 4, (h % 4) * P:(h % 4) * P + P], kh_(h, t * P, P), qh(h, t * P, P),
                                           start=True, stop=True)
                ins.then_inc(a_done, 1)

            def sums(n):
                t, a = n // 2, CH * (n % 2)
                if n:
                    if n == 1:
                        pe.wait_ge(s_ready, 1)
                    else:
                        pe.wait_ge(u_free, n - 1)
                pe.wait_ge(kt_evac, 2 * t + 2)
                for h in range(H):
                    ins = nc.tensor.matmul(ps[:, 2 + h // 4, (h % 4) * P:(h % 4) * P + P],
                                           tokens(zT)[a:a + CH, t, h * P:(h + 1) * P], vh(t, h, a, CH), start=True, stop=True)
                ins.then_inc(u_done, 1)

            def outputs(t):
                pe.wait_ge(at_evac, t + 1)
                pe.wait_ge(s_ready, 1 if t == 0 else 3)
                if t:
                    pe.wait_ge(o_sq, t)
                states = [work[6][:, 0:D], work[6][:, D:2 * D], work[7][:, 0:D]]
                for h in range(H):
                    o = ps[:, 6 + h // 4, (h % 4) * P:(h % 4) * P + P]
                    first = (h % 4 == 0)
                    ins = nc.tensor.matmul(o, tokens(tT)[:, t, h * P:(h + 1) * P], vh(t, h), start=first, stop=True,
                                           skip_group_check=True)
                    for half in range(2):
                        n = 2 * t + half
                        if n:
                            ins = nc.tensor.matmul(ps[CH * half:CH * half + CH, 6 + h // 4, (h % 4) * P:(h % 4) * P + P],
                                                   qh(h, n * CH, CH), states[n - 1][:, h * P:(h + 1) * P],
                                                   start=False, stop=True, skip_group_check=True)
                ins.then_inc(o_done, 1)

            pe.wait_ge(qk_ready, 2)
            turn_k(0)
            pe.wait_ge(group_free[0], 4)
            pe.wait_ge(group_free[1], 4)
            scores(0)
            sums(0)
            turn_k(1)
            scores(1)
            sums(1)
            outputs(0)
            sums(2)
            outputs(1)
            for t in range(TT):
                pe.wait_ge(on_ready, t + 1)
                for b in range(2):
                    if t:
                        pe.wait_ge(ot_lo, b + 1)
                    for i in range(4):
                        k = 4 * b + i
                        ins = nc.tensor.transpose(ps[:, b, i * P:(i + 1) * P], tokens(kT)[:, t, k * P:(k + 1) * P], ident[:])
                    ins.then_inc(ot_done, 1)
            pe.wait_ge(ot_lo, 4)
            for i in range(2):
                run_group(AT_WO + 2 * i, GR_WO + i, token_panel)

            turn_tokens(1, 4)
            for n, (kind, j, m) in enumerate(ffn_panels):
                c = AT_FFN + n
                if kind == "G":
                    if m == 0:
                        group_begins(GR_FFN + j)
                    if j == 0:
                        pe.wait_ge(lo_done, 4 + 2 * m + 2)
                    pe.wait_ge(lo_ready, c + 1)
                    for k in range(4):
                        for f in range(2):
                            for u in range(2):
                                o = ps[:, pair(GR_FFN + j) + f, u * S:(u + 1) * S]
                                ins = product(o, weights(c, k * 512 + u * 256 + f * P, P), acts(4 * m + k, 0, S),
                                              start=(m == 0 and k == 0 and u == 0), stop=(m == 1 and k == 3), share=True)
                    ins.then_inc(panel_used, 1)
                else:
                    pe.wait_ge(alo_ready, j + 1)
                    pe.wait_ge(lo_ready, c + 1)
                    for k in range(2):
                        for t in range(TT):
                            lhs = (a_hi[:, j % 2, k * S + t * P:k * S + (t + 1) * P], a_lo[:, j % 2, k * S + t * P:k * S + (t + 1) * P])
                            for i in range(2):
                                ins = product(ps[:, 2 * t + i, :], lhs, weights(c, k * D + i * 512, 512),
                                              start=(j == 0 and k == 0), stop=(j == FG - 1 and k == 1))
                    ins.then_inc(panel_used, 1)

            turn_tokens(2, 8)
            for g in range(GR_Q, GR_WO2):
                n = (g - GR_Q) // 2
                tiles = 8 if g == GR_Q else 12 if g == GR_Q + 2 else None
                run_group(AT_Q + 2 * (g - GR_Q), g, feature_panel if n < 2 else token_panel, tiles=tiles)

            def attn_scores(h):
                if h >= 2:
                    pe.wait_ge(sc_read, h - 1)
                nc.tensor.matmul(ps[:, h % 2, 0:P], qh(h, 0, P), kh_(h, 0, P), start=True, stop=True)
                nc.tensor.matmul(ps[:, h % 2, P:3 * P], qh(h, P, P), kh_(h, 0, S), start=True, stop=True).then_inc(sc_done, 1)

            pe.wait_ge(group_free[0], (GR_WO2 + 1) // 2)
            pe.wait_ge(group_free[1], GR_WO2 // 2)
            attn_scores(0)
            attn_scores(1)
            for h in range(H):
                pe.wait_ge(p_ready, h + 1)
                if h >= 2:
                    pe.wait_ge(pt_evac, h - 1)
                for q0, k0, at in ((0, 0, 0), (P, 0, P), (2 * P, 1, 2 * P)):
                    ins = nc.tensor.transpose(ps[:, 2 + h % 2, at:at + P],
                                              work[5][:, 512 * (h % 2) + q0:512 * (h % 2) + q0 + P], ident[:])
                ins.then_inc(pt_done, 1)
                if h + 2 < H:
                    attn_scores(h + 2)
                pe.wait_ge(pt_evac, h + 1)
                if h >= 2:
                    pe.wait_ge(ov_lo, h - 1)
                pt = work[5][:, 1024 + 512 * (h % 2):1024 + 512 * (h % 2) + 384]
                nc.tensor.matmul(ps[:, 4 + h % 2, 0:S], vh(0, h), pt[:, 0:S], start=True, stop=False, skip_group_check=True)
                nc.tensor.matmul(ps[:, 4 + h % 2, P:S], vh(1, h), pt[:, S:3 * P], start=False, stop=True,
                                 skip_group_check=True).then_inc(ov_done, 1)
            pe.wait_ge(ov_lo, H)
            for i in range(2):
                run_group(AT_WO2 + 2 * i, GR_WO2 + i, token_panel)

            turn_tokens(3, 12)
            pe.wait_ge(hf_ready, 4)
            pe.wait_ge(late_loaded, 48)
            for g in (GR_WO2, GR_WO2 + 1):
                pe.wait_ge(group_free[g % 2], g // 2 + 1)
            for t in range(TT):
                for k in range(KT):
                    ins = nc.tensor.matmul(ps[:, 4, t * E:(t + 1) * E], heads(qT)[:, k, t * P:(t + 1) * P], router[:, k, :],
                                           start=(k == 0), stop=(k == KT - 1))
            ins.then_inc(logits_done, 1)
            pe.wait_ge(picked, 1)
            nc.tensor.matmul(ps[:, 5, 0:E], earlier[:], route[:, 0, 7, :], start=True, stop=True)
            nc.tensor.matmul(ps[:, 5, E:2 * E], ones[:], route[:, 0, 7, :], start=True, stop=False)
            nc.tensor.matmul(ps[:, 5, E:2 * E], earlier[:], route[:, 1, 7, :], start=False, stop=True)
            nc.tensor.matmul(ps[:, 5, 2 * E:3 * E], ones[:], route[:, 0, 7, :], start=True, stop=False)
            nc.tensor.matmul(ps[:, 5, 2 * E:3 * E], ones[:], route[:, 1, 7, :], start=False, stop=True).then_inc(ranks_done, 1)

            def gather(passes):
                pe.wait_ge(m_sel, passes + 1)
                for b in range(2):
                    for i in range(4):
                        k = 4 * b + i
                        for t in range(TT):
                            ins = nc.tensor.matmul(ps[:, (7, 2)[b], i * P:(i + 1) * P], tokens(xn)[:, t, k * P:(k + 1) * P],
                                                   sel[:, t, :], start=(t == 0), stop=(t == TT - 1))
                    ins.then_inc(m_gath, 1)

            def scatter(p, q):
                t, i = q // 2, q % 2
                pe.wait_ge(m_out, p + 1)
                if q:
                    pe.wait_ge(m_add, p * 4 + q)
                nc.tensor.matmul(ps[:, 7, :], sel_T[:, t * P:(t + 1) * P], work[1][:, 512 * i:512 * i + 512],
                                 start=True, stop=True).then_inc(m_scat, 1)

            gather(0)

            def expert(p):
                def turn(j):
                    pe.wait_ge(m_act, p * EG + j + 1)
                    if j:
                        pe.wait_ge(m_alo, p * EG + j)
                    for i in range(4):
                        ins = nc.tensor.transpose(ps[:, 6, i * P:(i + 1) * P],
                                                  junk[:, 512 * (j % 2) + i * P:512 * (j % 2) + (i + 1) * P], ident[:])
                    ins.then_inc(m_turn, 1)

                pe.wait_ge(m_glo, p * 2 + 2)
                for c, (kind, j, m) in enumerate(moe_panels):
                    s = (MOE0 + c) % SPLIT_SLOTS
                    if kind == "D" and j == EG - 1 and m == 0:
                        turn(j)
                        pe.wait_ge(m_selT, p + 1)
                        gather(p + 1)
                    if kind == "G" and m == 0 and j >= 2:
                        pe.wait_ge(m_act, p * EG + j - 1)
                    if kind == "D" and m == 0:
                        pe.wait_ge(m_alo, p * EG + j + 1)
                        if j == 0:
                            pe.wait_ge(m_out, p + 1)
                    pe.wait_ge(lo_ready, p * NP + MOE0 + c + 1)
                    for k in range(2):
                        if kind == "G":
                            lhs = acts(2 * m + k, 0, P)
                            first, last = (m == 0 and k == 0), (m == 3 and k == 1)
                        else:
                            i0 = (2 * m + k) * P
                            lhs = (a_hi[:, j % 2, i0:i0 + P], a_lo[:, j % 2, i0:i0 + P])
                            first, last = (j == 0 and m == 0 and k == 0), (j == EG - 1 and m == 1 and k == 1)
                        for i in range(2):
                            bank = 2 * (j % 2) + i if kind == "G" else 4 + i
                            ins = product(ps[:, bank, :], lhs, weights(MOE0 + c, k * 1024 + i * 512, 512), start=first, stop=last)
                    ins.then_inc(panel_used, 1)
                    if kind == "G" and m == 1:
                        if j >= 1:
                            turn(j - 1)
                        if j < 2:
                            scatter(p, 2 * j)
                    if kind == "G" and m == 3:
                        if j < 2:
                            scatter(p, 2 * j + 1)
                        if j == 2:
                            pe.wait_ge(m_add, p * 4 + 4)
                            for t in range(TT):
                                ins = nc.tensor.transpose(ps[:, 7, t * P:(t + 1) * P], sel[:, t, :], ident[:])
                            ins.then_inc(m_selturn, 1)

            with pe.Fori(0, E) as p:
                expert(p)
            pe.wait_ge(info_ready, 1)
            extra = pe.value_load(info[0:1, 0:1], min_val=0, max_val=EXTRA)
            with pe.If(extra > 0):
                with pe.Fori(0, extra) as i:
                    expert(i + E)
            pe.wait_ge(m_glo, (extra + E) * 2 + 2)
            for q in range(4):
                scatter(extra + E, q)


_INS = ["x", "attn_norm", "ffn_norm", "hgrn_w_in", "hgrn_lb_logits", "hgrn_out_norm", "hgrn_w_o", "kv_norm",
        "w_kv", "moba_w_q", "moba_w_o", "ffn_w_gu", "ffn_w_down", "moe_router", "moe_w_gu", "moe_w_down", "final_norm"]


def kernel(**inputs):
    import concourse.bacc as bacc
    from concourse.bass_utils import run_bass_kernel_spmd

    nc = bacc.Bacc("TRN2", target_bir_lowering=False, num_devices=1)
    arrays, args = {}, []
    for name in _INS:
        a = np.ascontiguousarray(inputs[name])
        arrays[f"in_{name}"] = a
        args.append(nc.dram_tensor(f"in_{name}", a.shape, mybir.dt.from_np(a.dtype), kind="ExternalInput").ap())
    x = inputs["x"]
    args.append(nc.dram_tensor("out_0", x.shape, mybir.dt.from_np(np.dtype(x.dtype)), kind="ExternalOutput").ap())
    build_trunk(nc, *args)
    r = run_bass_kernel_spmd(nc, [arrays], core_ids=[0])
    return r.results[0]["out_0"]
```

```python
from contextlib import ExitStack

import numpy as np
import concourse.bass as bass
from concourse import mybir

F32 = mybir.dt.float32
F32R = mybir.dt.float32r
I32 = mybir.dt.int32
U32 = mybir.dt.uint32
ACT = mybir.ActivationFunctionType
ALU = mybir.AluOpType
AX_X = mybir.AxisListType.X

P = 128
EPS = 1e-6
RAW_SLOTS = 6
SPLIT_SLOTS = 3
WARM = (10, 12, 6, 10, 16)
PANEL = 2048


def build_trunk(nc, x, attn_norm, ffn_norm, hgrn_w_in, hgrn_lb_logits, hgrn_out_norm, hgrn_w_o,
                kv_norm, w_kv, moba_w_q, moba_w_o, ffn_w_gu, ffn_w_down,
                moe_router, moe_w_gu, moe_w_down, final_norm, out):
    _, S, D = x.shape
    TT = S // P
    KT = D // P
    H = KT
    CH = 64
    NCH = S // CH
    F = ffn_w_down.shape[1]
    E = moe_w_gu.shape[1]
    FE = moe_w_down.shape[2]
    FG = F // 256
    EG = FE // 512
    SCALE = float(P) ** -0.5
    SLOPES = [2.0 ** (-8.0 * (h + 1) / H) for h in range(H)]
    assert hgrn_w_in.shape[0] == 1 and moba_w_q.shape[0] == 1 and S == 256 and H == 8 and TT == 2
    EXTRA = (2 * S - E) // P
    EXTRA = min(EXTRA, 2 * S // (P + 1))
    NPASS = E + EXTRA

    def halves(v):
        k = v.shape[1] // 2
        return [("k", v[:, 0:k, :]), ("k", v[:, k:2 * k, :])]

    def square(w, c0, kh):
        return halves(w[kh * 512:(kh + 1) * 512, c0:c0 + 512].rearrange("(k p) c -> p k c", p=P))

    dense = []
    for c0 in (D, D + 512, 2 * D, 2 * D + 512, 0, 512, 3 * D, 3 * D + 512):
        dense += [square(hgrn_w_in[0], c0, kh) for kh in range(2)]
    AT_WO = len(dense)
    for c0 in (0, 512):
        dense += [square(hgrn_w_o[0], c0, kh) for kh in range(2)]
    AT_FFN = len(dense)
    gu_view = ffn_w_gu[0].rearrange("(k p) (u f) -> p k u f", p=P, u=2)
    down_view = ffn_w_down[0].rearrange("(k p) c -> p k c", p=P)
    ffn_order = [("G", 0)]
    for j in range(1, FG):
        ffn_order += [("G", j), ("D", j - 1)]
    ffn_order += [("D", FG - 1)]
    ffn_panels = []
    for kind, j in ffn_order:
        if kind == "G":
            for kh in range(2):
                dense.append([("u", gu_view[:, 4 * kh:4 * kh + 4, u, j * 256:(j + 1) * 256]) for u in range(2)])
                ffn_panels.append((kind, j, kh))
        else:
            dense.append(halves(down_view[:, 2 * j:2 * j + 2, :]))
            ffn_panels.append((kind, j, 0))
    AT_Q = len(dense)
    for w, c0 in ((moba_w_q[0], 0), (w_kv, 0), (w_kv, D)):
        for c in (c0, c0 + 512):
            dense += [square(w, c, kh) for kh in range(2)]
    AT_KV = AT_Q + 4
    AT_V = AT_KV + 4
    AT_WO2 = len(dense)
    for c0 in (0, 512):
        dense += [square(moba_w_o[0], c0, kh) for kh in range(2)]
    MOE0 = len(dense)
    order = [("G", 0)]
    for j in range(1, EG):
        order += [("G", j), ("D", j - 1)]
    order += [("D", EG - 1)]
    moe_panels = [(k, j, m) for k, j in order for m in range(4 if k == "G" else 2)]
    NP = len(moe_panels)
    ffn_end = {(k, j): n + 1 for n, (k, j, _) in enumerate(ffn_panels)}
    moe_end = {(k, j): n + 1 for n, (k, j, _) in enumerate(moe_panels)}
    assert NP % RAW_SLOTS == 0 and NP % SPLIT_SLOTS == 0

    GR_IN, GR_WO = 0, 8
    GR_FFN = GR_WO + 2
    GR_Q = GR_FFN
    GR_WO2 = GR_Q + 6
    GROUPS = GR_WO2 + 2

    ctx = ExitStack()
    with ctx:
        def sb(name, shape, dt=F32):
            return ctx.enter_context(nc.sbuf_tensor(name, shape, dt))

        def sem(name):
            return ctx.enter_context(nc.semaphore(name))

        w_raw = sb("w_raw", [P, RAW_SLOTS, PANEL])
        w_hi = sb("w_hi", [P, SPLIT_SLOTS, PANEL], F32R)
        w_lo = sb("w_lo", [P, SPLIT_SLOTS, PANEL], F32R)
        h_hi = sb("h_hi", [P, KT, S], F32R)
        h_lo = sb("h_lo", [P, KT, S], F32R)
        a_hi = sb("a_hi", [P, 2, 512], F32R)
        a_lo = sb("a_lo", [P, 2, 512], F32R)
        x_res = sb("x_res", [P, TT, D])
        junk = sb("junk", [P, D])
        gu = junk[:].rearrange("p (n u f s) -> p n u f s", n=2, u=1, s=S)
        work = [sb(f"work{n}", [P, 2048]) for n in range(6)]
        with nc.sbuf_tensor("work6", [P, 2048], F32) as work6, nc.sbuf_tensor("work7", [P, 2048], F32) as work7:
            work += [work6, work7]
        rounded6, rounded7 = sb("rounded6", [P, 2048], F32R), sb("rounded7", [P, 2048], F32R)
        qT, kT, zT, tT = work[0], work[1], work[2], work[3]
        v_tm, g_tm = work[4], work[5]
        xn = work[6]
        xn_hi, xn_lo = rounded7[:], rounded6[:]
        router_x = work[6]
        early_raw = [work[n][:] for n in (0, 2, 3, 4)]
        moe_gain = work[5][:, D:2 * D]
        final_gain = work[1][:, D:2 * D]
        bias = [work[2 + h // 5][:, 384 * (h % 5):384 * (h % 5) + 384] for h in range(H)]
        q_hi, q_lo = (w[:].rearrange("p (h s) -> p h s", h=H) for w in (rounded6, rounded7))
        probs = [work[5][:, 0:384], work[5][:, 512:896], junk[:, 0:384], junk[:, 512:896]]
        turned_p = [(work[7], work[6])[h // 5][:, 384 * (h % 5):384 * (h % 5) + 384] for h in range(H)]
        ident = sb("ident", [P, P])
        chunk_mask = sb("chunk_mask", [P, P])
        earlier = sb("earlier", [P, P])
        ones = sb("ones", [P, P])
        slot_id = sb("slot_id", [P, P])
        expert_id = sb("expert_id", [P, E])
        alibi = work[0][:, 0:3 * P]
        scan_keep = sb("scan_keep", [P, NCH, CH])
        gain_rows = sb("gain_rows", [6 * KT, P])
        gains = sb("gains", [P, 6 * KT])
        router = sb("router", [P, KT, E])
        sumsq = sb("sumsq", [P, 5, TT])
        mean_sq = sb("mean_sq", [P, 5, TT])
        std = sb("std", [P, 5, TT])
        rstd = sb("rstd", [P, 5, TT])
        rms_row = sb("rms_row", [P, S])
        diag = rms_row[:].rearrange("p (t s) -> p t s", t=TT)
        b_ref = sb("b_ref", [P, H, NCH])
        b_last = sb("b_last", [P, H, NCH])
        alpha = sb("alpha", [P, H, NCH])
        head_ms = sb("head_ms", [P, TT, H])
        head_std = sb("head_std", [P, TT, H])
        head_rstd = sb("head_rstd", [P, TT, H])
        soft = sb("soft", [P, H, 8])
        sel = sb("sel", [P, TT, P], F32R)
        sel_f = sel[:].bitcast(F32)
        sel_T = sb("sel_T", [P, S])
        route = sb("route", [P, TT, 12, 8])
        route_u = sb("route_u", [P, TT, 8], U32)
        pass_rank = sb("pass_rank", [P, TT, NPASS + 2])
        pass_gate = sb("pass_gate", [P, TT, NPASS + 2])
        over = sb("over", [P, 8, 8])
        picked_rank = sb("picked_rank", [P, TT, 8])
        picked_gate = sb("picked_gate", [P, TT, 8])
        info_f = sb("info_f", [P, 4])
        info = sb("info", [P, 4], I32)
        ps = ctx.enter_context(nc.psum_tensor("ps", [P, 8, 512], F32))

        CONSTS = 7
        GAIN_ATTN0, GAIN_ATTN1, GAIN_FFN0, GAIN_FFN1, GAIN_OUT, GAIN_KV = (n * KT for n in range(6))

        early_landed = [sem(f"early_landed{n}") for n in range(len(early_raw))]
        raw_landed = [sem(f"raw_landed{s}") for s in range(RAW_SLOTS)]
        hi_ready = sem("hi_ready")
        lo_ready = sem("lo_ready")
        panel_used = sem("panel_used")
        x_loaded = sem("x_loaded")
        attn_gains_loaded = sem("attn_gains_loaded")
        gains_loaded = sem("gains_loaded")
        late_loaded = sem("late_loaded")
        final_loaded = sem("final_loaded")
        consts = sem("consts")
        const_step = sem("const_step")
        gains_turned = sem("gains_turned")
        gains_ready = sem("gains_ready")
        act_step = sem("act_step")
        dve_step = sem("dve_step")
        sq_done = sem("sq_done")
        ms_ready = sem("ms_ready")
        std_ready = sem("std_ready")
        tr_done = sem("tr_done")
        diag_ready = sem("diag_ready")
        row_done = sem("row_done")
        row_ready = sem("row_ready")
        scaled = sem("scaled")
        down_half = sem("down_half")
        bias_ready = sem("bias_ready")
        hi_done = sem("hi_done")
        lo_done = sem("lo_done")
        group_free = [sem("group_free0"), sem("group_free1")]
        act_read = sem("act_read")
        sig_ready = sem("sig_ready")
        ln_ready = sem("ln_ready")
        q_silu = sem("q_silu")
        k_ready = sem("k_ready")
        q_ready = sem("q_ready")
        scores_clear = sem("scores_clear")
        act_ready = sem("act_ready")
        arg_ready = sem("arg_ready")
        e1_ready = sem("e1_ready")
        e2_ready = sem("e2_ready")
        alpha_ready = sem("alpha_ready")
        alpha_arg = sem("alpha_arg")
        qk_ready = sem("qk_ready")
        kt_done = sem("kt_done")
        kt_evac = sem("kt_evac")
        a_done = sem("a_done")
        at_evac = sem("at_evac")
        u_done = sem("u_done")
        u_free = sem("u_free")
        s_ready = sem("s_ready")
        o_done = sem("o_done")
        o_sq = sem("o_sq")
        o_ms = sem("o_ms")
        o_std = sem("o_std")
        on_ready = sem("on_ready")
        ot_done = sem("ot_done")
        ot_hi = sem("ot_hi")
        ot_lo = sem("ot_lo")
        x_added = sem("x_added")
        silu_ready = sem("silu_ready")
        ahi_ready = sem("ahi_ready")
        alo_ready = sem("alo_ready")
        sc_done = sem("sc_done")
        max_ready = sem("max_ready")
        exp_ready = sem("exp_ready")
        p_ready = sem("p_ready")
        pt_done = sem("pt_done")
        pt_evac = sem("pt_evac")
        ov_done = sem("ov_done")
        ov_hi = sem("ov_hi")
        ov_lo = sem("ov_lo")
        h_ready = sem("h_ready")
        xn_rounded = sem("xn_rounded")
        xn_split = sem("xn_split")
        hf_ready = sem("hf_ready")
        logits_done = sem("logits_done")
        gap_ready = sem("gap_ready")
        gate_exp = sem("gate_exp")
        picked = sem("picked")
        ranks_done = sem("ranks_done")
        info_ready = sem("info_ready")
        m_silu = sem("m_silu")
        m_act = sem("m_act")
        m_turn = sem("m_turn")
        m_ahi = sem("m_ahi")
        m_alo = sem("m_alo")
        m_out = sem("m_out")
        m_scat = sem("m_scat")
        m_add = sem("m_add")
        m_selturn = sem("m_selturn")
        m_selT = sem("m_selT")
        m_sel = sem("m_sel")
        m_gath = sem("m_gath")
        m_ghi = sem("m_ghi")
        m_glo = sem("m_glo")
        out_ready = sem("out_ready")
        out_stored = sem("out_stored")

        block = ctx.enter_context(nc.Block())

        def heads(t):
            return t[:].rearrange("p (h s) -> p h s", h=H)

        def tokens(t):
            return t[:].rearrange("p (t d) -> p t d", t=TT)

        def chunks(t):
            return t[:].rearrange("p (n c) -> p n c", c=CH)

        def pair(g):
            return 4 + 2 * (g % 2)

        BEFORE_EARLY = MOE0 + SPLIT_SLOTS - 1 + RAW_SLOTS - 1
        EARLY = [MOE0 + SPLIT_SLOTS + 8 * n for n in range(len(early_raw))]

        def is_early(c, last):
            return last and c in EARLY

        def raw(c, last):
            return early_raw[EARLY.index(c)] if is_early(c, last) else w_raw[:, c % RAW_SLOTS, :]

        def landed(eng, c, passes=0, last=False):
            if is_early(c, last):
                eng.wait_ge(early_landed[EARLY.index(c)], 32)
            else:
                cycles = c // RAW_SLOTS + 1
                if last:
                    cycles -= sum(e < c and (c - e) % RAW_SLOTS == 0 for e in EARLY)
                eng.wait_ge(raw_landed[c % RAW_SLOTS], passes * (32 * (NP // RAW_SLOTS)) + 32 * cycles)

        def split_hi(act, c, passes=0, last=False):
            if last and c >= MOE0 + NP:
                return
            landed(act, c, passes, last)
            if c >= SPLIT_SLOTS:
                act.wait_ge(panel_used, passes * NP + c - SPLIT_SLOTS + 1)
            nc.scalar.activation(w_hi[:, c % SPLIT_SLOTS, :], raw(c, last), ACT.Copy).then_inc(hi_ready, 1)

        def split_lo(dve, c, passes=0, last=False):
            if last and c >= MOE0 + NP:
                return
            dve.wait_ge(hi_ready, passes * NP + c + 1)
            nc.vector.tensor_tensor(w_lo[:, c % SPLIT_SLOTS, :], raw(c, last),
                                    w_hi[:, c % SPLIT_SLOTS, :].bitcast(F32), ALU.subtract).then_inc(lo_ready, 1)

        def moe_gu(e, j, m):
            v = moe_w_gu[0, e].rearrange("(k p) (u f) -> p k u f", p=P, u=2)
            return [("u", v[:, 2 * m:2 * m + 2, u, j * 512:(j + 1) * 512]) for u in range(2)]

        def moe_down(e, j, m):
            v = moe_w_down[0, e].rearrange("(k p) c -> p k c", p=P)
            return halves(v[:, 4 * j + 2 * m:4 * j + 2 * m + 2, :])

        @block.sync
        def _(sp):
            def load(c, src, passes=0, last=False):
                if is_early(c, last):
                    if c == EARLY[0]:
                        sp.wait_ge(ov_done, H)
                elif c >= RAW_SLOTS:
                    back = RAW_SLOTS
                    while is_early(c - back, last):
                        back += RAW_SLOTS
                    sp.wait_ge(lo_ready, passes * NP + c - back + 1)
                done = early_landed[EARLY.index(c)] if is_early(c, last) else raw_landed[c % RAW_SLOTS]
                for n, (cut, part) in enumerate(src):
                    k = part.shape[1]
                    if cut == "k":
                        dst = raw(c, last).rearrange("p (n k f) -> p n k f", n=2, k=k)[:, n]
                    else:
                        dst = raw(c, last).rearrange("p (k u f) -> p k u f", k=k, u=2)[:, :, n]
                    sp.dma_start(dst, part).then_inc(done, 16)

            sp.dma_start(x_res[:], x.rearrange("b (t p) d -> p (b t) d", p=P)).then_inc(x_loaded, 16)
            for c, src in enumerate(dense):
                load(c, src)

            def panel(c, e, passes, last=False):
                kind, j, m = moe_panels[c - MOE0]
                load(c, moe_gu(e, j, m) if kind == "G" else moe_down(e, j, m), passes, last)

            def expert(e, passes, last=False):
                for c in range(MOE0, MOE0 + NP):
                    if not is_early(c, last):
                        panel(c, e, passes, last)
                    if isinstance(passes, int) and c == BEFORE_EARLY:
                        for early in EARLY:
                            panel(early, E - 1, 0, True)

            expert(0, 0)
            with sp.Fori(1, E - 1) as e:
                expert(e, e)
            sp.wait_ge(info_ready, 1)
            extra = sp.value_load(info[0:1, 0:1], min_val=0, max_val=EXTRA)
            with sp.If(extra > 0):
                with sp.Fori(0, extra) as i:
                    e = sp.value_load(info[0:1, bass.ds(i + 1, 1)], min_val=0, max_val=E - 1)
                    expert(e, i + (E - 1))
            expert(E - 1, extra + (E - 1), last=True)
            for t in range(TT):
                sp.wait_ge(out_ready, t + 1)
                sp.dma_start(out[0, t * P:(t + 1) * P, :], tokens(xn)[:, t, :]).then_inc(out_stored, 16)
            sp.wait_ge(out_stored, 16 * TT)

        @block.gpsimd
        def _(pool):
            nc.gpsimd.memset(ident[:], 0.0).then_inc(const_step, 1)
            pool.wait_ge(const_step, 1)
            nc.gpsimd.affine_select(ident[:], ident[:], [[-1, P]], ALU.not_equal, 1.0, base=0,
                                    channel_multiplier=1).then_inc(consts, 1)
            nc.gpsimd.memset(ones[:], 1.0).then_inc(consts, 1)
            nc.gpsimd.memset(chunk_mask[:], 1.0).then_inc(const_step, 1)
            nc.gpsimd.memset(earlier[:], 1.0).then_inc(const_step, 1)
            nc.gpsimd.memset(scan_keep[:], 1.0).then_inc(const_step, 1)
            nc.gpsimd.iota(slot_id[:], [[1, P]], base=0, channel_multiplier=0,
                           allow_small_or_imprecise_dtypes=True).then_inc(consts, 1)
            nc.gpsimd.iota(expert_id[:], [[1, E]], base=0, channel_multiplier=0,
                           allow_small_or_imprecise_dtypes=True).then_inc(consts, 1)
            pool.wait_ge(const_step, 4)
            nc.gpsimd.affine_select(chunk_mask[:], chunk_mask[:], [[1, P]], ALU.is_ge, 0.0, base=0,
                                    channel_multiplier=-1).then_inc(const_step, 1)
            nc.gpsimd.affine_select(earlier[:], earlier[:], [[1, P]], ALU.is_gt, 0.0, base=0,
                                    channel_multiplier=-1).then_inc(consts, 1)
            nc.gpsimd.memset(scan_keep[:, :, 0:1], 0.0).then_inc(consts, 1)
            pool.wait_ge(const_step, 5)
            nc.gpsimd.memset(chunk_mask[0:CH, CH:P], 0.0).then_inc(consts, 1)
            pool.dma_start(router[:], moe_router[0].rearrange("(k p) e -> p k e", p=P)).then_inc(late_loaded, 16)
            pool.wait_ge(q_ready, 2)
            nc.gpsimd.memset(tT[:], 0.0).then_inc(scores_clear, 1)
            pool.wait_ge(ot_done, 4)
            pool.dma_start(moe_gain, ffn_norm[1].partition_broadcast(P)).then_inc(late_loaded, 16)
            nc.gpsimd.iota(alibi[:, 0:P], [[1, P]], base=0, channel_multiplier=-1,
                           allow_small_or_imprecise_dtypes=True).then_inc(const_step, 1)
            nc.gpsimd.iota(alibi[:, P:3 * P], [[1, 2 * P]], base=-P, channel_multiplier=-1,
                           allow_small_or_imprecise_dtypes=True).then_inc(const_step, 1)
            pool.wait_ge(const_step, 7)
            nc.gpsimd.affine_select(alibi[:, 0:P], alibi[:, 0:P], [[-1, P]], ALU.is_ge, -1e30, base=0,
                                    channel_multiplier=1).then_inc(const_step, 1)
            nc.gpsimd.affine_select(alibi[:, P:3 * P], alibi[:, P:3 * P], [[-1, 2 * P]], ALU.is_ge, -1e30, base=P,
                                    channel_multiplier=1).then_inc(const_step, 1)
            pool.wait_ge(const_step, 9)
            for h in range(H):
                ins = nc.gpsimd.tensor_scalar(bias[h], alibi[:], SLOPES[h] / SCALE, None, ALU.mult)
            ins.then_inc(bias_ready, 1)
            pool.wait_ge(late_loaded, 32)
            pool.wait_ge(ov_done, H)
            pool.dma_start(final_gain, final_norm.partition_broadcast(P)).then_inc(final_loaded, 16)
            pool.wait_ge(final_loaded, 16)

        @block.scalar
        def _(act):
            for n, (src, lines) in enumerate(((attn_norm, 2 * KT), (ffn_norm, 2 * KT), (hgrn_out_norm, KT))):
                at = (0, 2 * KT, 4 * KT)[n]
                act.dma_start(gain_rows[at:at + lines, :], src.rearrange("l (k p) -> (l k) p", p=P)).then_inc(
                    attn_gains_loaded if n == 0 else gains_loaded, 16)
            act.dma_start(gain_rows[5 * KT:6 * KT, :], kv_norm.rearrange("(k p) -> k p", p=P)).then_inc(gains_loaded, 16)

            def norm_squares(n):
                for t in range(TT):
                    nc.scalar.activation(junk[:], x_res[:, t, :], ACT.Square,
                                         accum_out=sumsq[:, n, t:t + 1]).then_inc(sq_done, 1)
                    act.wait_ge(sq_done, TT * n + t + 1)

            def norm_root(n):
                act.wait_ge(ms_ready, n + 1)
                nc.scalar.activation(std[:, n, :], mean_sq[:, n, :], ACT.Sqrt).then_inc(std_ready, 1)

            def norm_stats(n):
                norm_squares(n)
                norm_root(n)

            def norm_hi(gain, tr, half, hi=h_hi):
                for b in (2 * half, 2 * half + 1):
                    act.wait_ge(tr_done, tr + b + 1)
                    for i in range(2):
                        ins = nc.scalar.activation(hi[:, 2 * b + i, :], ps[:, b, i * S:(i + 1) * S], ACT.Copy,
                                                   scale=gains[:, gain + 2 * b + i:gain + 2 * b + i + 1])
                    ins.then_inc(hi_done, 1)

            def tokens_out(c, g, i, to, norm):
                act.wait_ge(std_ready, norm + 1)
                act.wait_ge(diag_ready, norm + 1)
                act.wait_ge(panel_used, c + 1)
                for t in range(TT):
                    ins = nc.scalar.activation(tokens(to)[:, t, 512 * i:512 * i + 512], ps[:, pair(g) + t, :], ACT.Copy,
                                               scale=rstd[:, norm, t:t + 1])
                ins.then_inc(group_free[g % 2], 1)

            act.wait_ge(gains_turned, 1)
            nc.scalar.activation(gains[:, 0:2 * KT], ps[:, 7, 0:2 * KT], ACT.Copy).then_inc(gains_ready, 1)
            act.wait_ge(gains_ready, 1)
            for half in range(2):
                norm_hi(GAIN_ATTN0, 0, half)
                split_hi(act, half)
            norm_squares(0)
            split_hi(act, 2)
            norm_root(0)
            act.wait_ge(gains_turned, 2)
            nc.scalar.activation(gains[:, 2 * KT:6 * KT], ps[:, 7, 2 * KT:6 * KT], ACT.Copy).then_inc(gains_ready, 1)
            act.wait_ge(gains_ready, 2)

            for c in range(AT_WO):
                if c == AT_WO - 1:
                    for t in range(TT):
                        act.wait_ge(o_done, t + 1)
                        nc.scalar.activation(tokens(zT)[:, t, :], ps[:, 2 * t:2 * t + 2, :].rearrange("p b f -> p (b f)"),
                                             ACT.Square).then_inc(o_sq, 1)
                    for t in range(TT):
                        act.wait_ge(o_ms, t + 1)
                        nc.scalar.activation(head_std[:, t, :], head_ms[:, t, :], ACT.Sqrt).then_inc(o_std, 1)
                else:
                    split_hi(act, c + SPLIT_SLOTS)
                g = c // 2
                half = slice(1024 * (g % 2), 1024 * (g % 2) + 1024)
                if c in (1, 3):
                    act.wait_ge(scaled, g + 1)
                    nc.scalar.activation(kT[:, half], zT[:, half], ACT.Sigmoid, scale=-1.0)
                    nc.scalar.activation(tT[:, half], zT[:, half], ACT.Abs).then_inc(sig_ready, 1)
                    act.wait_ge(sig_ready, 2 * g + 1)
                    nc.scalar.activation(tT[:, half], tT[:, half], ACT.Sigmoid).then_inc(sig_ready, 1)
                if c == 3:
                    act.wait_ge(sig_ready, 4)
                    nc.scalar.activation(tT[:], tT[:], ACT.Ln).then_inc(ln_ready, 1)
                if c in (5, 7):
                    tokens_out(c, g, g % 2, v_tm, 0)
                if c == 7:
                    act.wait_ge(arg_ready, 1)
                    nc.scalar.activation(tT[:], zT[:], ACT.Exp).then_inc(e1_ready, 1)
                    act.wait_ge(e1_ready, 1)
                    nc.scalar.activation(zT[:], zT[:], ACT.Exp, scale=-1.0).then_inc(e2_ready, 1)
                    nc.scalar.activation(alpha[:], alpha[:], ACT.Exp).then_inc(alpha_ready, 1)
                if c in (9, 11):
                    act.wait_ge(scaled, g - 1)
                    nc.scalar.activation(qT[:, half], qT[:, half], ACT.Silu).then_inc(q_silu, 1)
                if c in (10, 11):
                    for n in (2 * (c - 10), 2 * (c - 10) + 1):
                        act.wait_ge(kt_done, n + 1)
                        nc.scalar.activation(tokens(zT)[:, n // 2, (n % 2) * 512:(n % 2) * 512 + 512], ps[:, n % 2, :],
                                             ACT.Copy).then_inc(kt_evac, 1)
                if c in (13, 15):
                    act.wait_ge(panel_used, c + 1)
                    for t in range(TT):
                        ins = nc.scalar.activation(tokens(g_tm)[:, t, 512 * (g % 2):512 * (g % 2) + 512],
                                                   ps[:, pair(g) + t, :], ACT.Silu, scale=rstd[:, 0, t:t + 1])
                    ins.then_inc(group_free[g % 2], 1)

            def outputs_hi(b):
                for t in range(TT):
                    act.wait_ge(ot_done, 2 * b + t + 1)
                    for i in range(4):
                        k = 4 * b + i
                        ins = nc.scalar.activation(h_hi[:, k, t * P:(t + 1) * P], ps[:, 4 + 2 * b + t, i * P:(i + 1) * P], ACT.Copy,
                                                   scale=gains[:, GAIN_OUT + k:GAIN_OUT + k + 1])
                    ins.then_inc(ot_hi, 1)

            outputs_hi(0)
            outputs_hi(1)
            split_hi(act, AT_WO - 1 + SPLIT_SLOTS)
            for c in range(AT_WO, AT_FFN):
                if c == AT_FFN - 2:
                    norm_hi(GAIN_FFN0, 4, 0)
                if c == AT_FFN - 1:
                    norm_hi(GAIN_FFN0, 4, 1)
                split_hi(act, c + SPLIT_SLOTS)

            act.wait_ge(group_free[1], (GR_WO + 1) // 2 + 1)
            norm_stats(1)
            for n, (kind, j, m) in enumerate(ffn_panels):
                last_g = kind == "G" and j == FG - 1 and m == 1
                if kind == "D" and j == FG - 1:
                    norm_hi(GAIN_ATTN1, 8, 0, q_hi)
                    act.wait_ge(x_added, 4)
                    norm_squares(2)
                    norm_hi(GAIN_ATTN1, 8, 1, q_hi)
                if not last_g:
                    split_hi(act, AT_FFN + n + SPLIT_SLOTS)
                if kind == "G" and m == 1:
                    gate = gu[:, j % 2, 0]
                    act.wait_ge(scaled, 4 + j + 1)
                    nc.scalar.activation(gate, gate, ACT.Silu).then_inc(silu_ready, 1)
                    act.wait_ge(act_ready, j + 1)
                    if j >= 2:
                        act.wait_ge(panel_used, AT_FFN + ffn_end["D", j - 2])
                    nc.scalar.activation(a_hi[:, j % 2, :], gu[:, j % 2, 0].rearrange("p f s -> p (f s)"), ACT.Copy).then_inc(ahi_ready, 1)
                if last_g:
                    split_hi(act, AT_FFN + n + SPLIT_SLOTS)

            norm_root(2)

            def probabilities(h):
                act.wait_ge(max_ready, h + 1)
                p = probs[h % 4]
                for t in range(TT):
                    part = p[:, 0:P] if t == 0 else p[:, P:3 * P]
                    ins = nc.scalar.activation(part, part, ACT.Exp, bias=soft[:, h, 2 + t:3 + t], scale=SCALE,
                                               accum_out=soft[:, h, 4 + t:5 + t])
                ins.then_inc(exp_ready, 1)

            def turned_out(h):
                act.wait_ge(pt_done, h + 1)
                nc.scalar.activation(turned_p[h], ps[:, 2 + h % 2, 0:384], ACT.Copy).then_inc(pt_evac, 1)

            for c in range(AT_Q, AT_WO2):
                if c > AT_V:
                    turned_out(2 * (c - AT_V) - 2)
                    turned_out(2 * (c - AT_V) - 1)
                if AT_V - 1 <= c < AT_WO2 - 1:
                    probabilities(2 * (c - AT_V) + 2)
                    probabilities(2 * (c - AT_V) + 3)
                if c < AT_WO2 - 1:
                    split_hi(act, c + SPLIT_SLOTS)
                if c in (AT_Q, AT_Q + 1):
                    act.wait_ge(lo_done, 12)
                    norm_hi(GAIN_KV, 8, c - AT_Q)
                if c in (AT_V + 1, AT_V + 3):
                    i = (c - AT_V) // 2
                    tokens_out(c, GR_Q + 4 + i, i, v_tm, 2)
            turned_out(H - 2)
            turned_out(H - 1)
            for h in range(H):
                act.wait_ge(ov_done, h + 1)
                nc.scalar.activation(h_hi[:, h, :], ps[:, 4 + h % 4, 0:S], ACT.Copy).then_inc(ov_hi, 1)
            split_hi(act, AT_WO2 - 1 + SPLIT_SLOTS)
            def router_tokens(half):
                for b in (2 * half, 2 * half + 1):
                    act.wait_ge(tr_done, 12 + b + 1)
                    for i in range(2):
                        k = 2 * b + i
                        ins = nc.scalar.activation(heads(router_x)[:, k, :], ps[:, b, i * S:(i + 1) * S], ACT.Copy,
                                                   scale=gains[:, GAIN_FFN1 + k:GAIN_FFN1 + k + 1])
                    ins.then_inc(hf_ready, 1)

            for c in range(AT_WO2, MOE0):
                if c == MOE0 - 2:
                    router_tokens(0)
                if c == MOE0 - 1:
                    router_tokens(1)
                    norm_root(3)
                split_hi(act, c + SPLIT_SLOTS)


            def gather_hi(passes):
                for b in range(2):
                    act.wait_ge(m_gath, 2 * passes + b + 1)
                    nc.scalar.activation(h_hi[:, 4 * b:4 * b + 4, 0:P],
                                         ps[:, (7, 2)[b], :].rearrange("p (k s) -> p k s", k=4), ACT.Copy).then_inc(m_ghi, 1)

            for t in range(TT):
                act.wait_ge(h_ready, t + 1)
                cols = slice(t * D, (t + 1) * D)
                nc.scalar.activation(xn_hi[:, cols], xn[:, cols], ACT.Copy).then_inc(xn_rounded, 1)
            gather_hi(0)

            def expert(p, last=False):
                def turned_hi(j):
                    act.wait_ge(m_turn, p * EG + j + 1)
                    act.wait_ge(panel_used, p * NP + MOE0 + (moe_end["D", j - 2] if j >= 2 else 0))
                    nc.scalar.activation(a_hi[:, j % 2, :], ps[:, 6, :], ACT.Copy).then_inc(m_ahi, 1)

                for c, (kind, j, m) in enumerate(moe_panels):
                    if kind == "D" and j == EG - 2 and m == 0:
                        turned_hi(EG - 1)
                    if kind == "D" and j == EG - 1 and m == 0 and not last:
                        gather_hi(p + 1)
                    if c == NP - 1:
                        act.wait_ge(panel_used, p * NP + MOE0 + NP)
                        nc.scalar.activation(work[1][:, 0:D], ps[:, 4:6, :].rearrange("p b f -> p (b f)"), ACT.Copy).then_inc(m_out, 1)
                    if kind == "G" and m == 3:
                        act.wait_ge(panel_used, p * NP + MOE0 + c + 1)
                        if j >= 2:
                            act.wait_ge(m_turn, p * EG + j - 1)
                        nc.scalar.activation(junk[:, 512 * (j % 2):512 * (j % 2) + 512], ps[:, 2 * (j % 2), :],
                                             ACT.Silu).then_inc(m_silu, 1)
                    split_hi(act, MOE0 + c + SPLIT_SLOTS, p, last)
                    if isinstance(p, int) and c == 0:
                        act.wait_ge(gap_ready, 1)
                        nc.scalar.activation(route[:, :, 3, 0:1], route[:, :, 2, 0:1], ACT.Exp).then_inc(gate_exp, 1)
                    if kind == "G" and m == 1 and j >= 1:
                        turned_hi(j - 1)
                    if kind == "G" and m == 3:
                        if j == 2:
                            act.wait_ge(m_selturn, p + 1)
                            nc.scalar.activation(sel_T[:], ps[:, 7, 0:S], ACT.Copy).then_inc(m_selT, 1)

            expert(0)
            with act.Fori(1, E - 1) as p:
                expert(p)
            act.wait_ge(info_ready, 1)
            extra = act.value_load(info[0:1, 0:1], min_val=0, max_val=EXTRA)
            with act.If(extra > 0):
                with act.Fori(0, extra) as i:
                    expert(i + (E - 1))
            expert(extra + (E - 1), last=True)
            nc.scalar.activation(head_std[:, 0, 0:1], mean_sq[:, 3, 0:1], ACT.Sqrt).then_inc(act_step, 1)
            for t in range(TT):
                act.wait_ge(m_add, (extra + (E - 1)) * 4 + 2 * t + 2)
                nc.scalar.activation(junk[:], x_res[:, t, :], ACT.Square, accum_out=sumsq[:, 4, t:t + 1]).then_inc(sq_done, 1)
                act.wait_ge(ms_ready, 5 + t)
                nc.scalar.activation(std[:, 4, t:t + 1], mean_sq[:, 4, t:t + 1], ACT.Sqrt).then_inc(std_ready, 1)

        @block.vector
        def _(dve):
            steps = [0]

            def link(ins):
                steps[0] += 1
                ins.then_inc(dve_step, 1)
                dve.wait_ge(dve_step, steps[0])

            def norm_mean(n):
                dve.wait_ge(sq_done, TT * n + TT)
                nc.vector.tensor_scalar(mean_sq[:, n, :], sumsq[:, n, :], 1.0 / D, EPS, ALU.mult, ALU.add).then_inc(ms_ready, 1)

            def norm_scale(n, ms=True):
                if ms:
                    norm_mean(n)
                dve.wait_ge(std_ready, n + 1)
                link(nc.vector.reciprocal(rstd[:, n, :], std[:, n, :]))

            def norm_row(n, bank=0, ms=True):
                norm_scale(n, ms)
                for t in range(TT):
                    ins = nc.vector.tensor_scalar(diag[:, t, :], ident[:], rstd[:, n, t:t + 1], None, ALU.mult)
                ins.then_inc(diag_ready, 1)
                dve.wait_ge(row_done, n + 1)
                nc.vector.tensor_copy(rms_row[:], ps[:, bank, 0:S]).then_inc(row_ready, 1)
                dve.wait_ge(row_ready, n + 1)

            def norm_lo(gain, done, half, hi=h_hi, lo=h_lo):
                for b in (2 * half, 2 * half + 1):
                    dve.wait_ge(hi_done, done + b + 1)
                    for i in range(2):
                        k = 2 * b + i
                        ins = nc.vector.scalar_tensor_tensor(lo[:, k, :], ps[:, b, i * S:(i + 1) * S],
                                                             gains[:, gain + k:gain + k + 1], hi[:, k, :].bitcast(F32),
                                                             ALU.mult, ALU.subtract)
                    ins.then_inc(lo_done, 1)

            def add_group(c, g, i):
                dve.wait_ge(panel_used, c + 1)
                for t in range(TT):
                    xs = x_res[:, t, 512 * i:512 * i + 512]
                    ins = nc.vector.tensor_tensor(xs, xs, ps[:, pair(g) + t, :], ALU.add)
                ins.then_inc(group_free[g % 2], 1)

            def features_out(c, g, i, to):
                dve.wait_ge(panel_used, c + 1)
                for b in range(2):
                    part = heads(to)[:, 4 * i + 2 * b:4 * i + 2 * b + 2, :]
                    ins = nc.vector.tensor_tensor(part, ps[:, pair(g) + b, :].rearrange("p (f s) -> p f s", s=S),
                                                  rms_row[:].unsqueeze(1).broadcast_to([P, 2, S]), ALU.mult)
                    if b == 0:
                        continue
                    ins.then_inc(group_free[g % 2], 1)

            dve.wait_ge(gains_ready, 1)
            for half in range(2):
                norm_lo(GAIN_ATTN0, 0, half)
                split_lo(dve, half)
            split_lo(dve, 2)
            dve.wait_ge(consts, CONSTS)
            norm_row(0)

            def by_head(a):
                return a.rearrange("p (h v) -> p h v", h=H)

            def carry(n):
                return alpha[:, :, n:n + 1].broadcast_to([P, H, P])

            states = [work[6][:, 0:D], work[6][:, D:2 * D], work[7][:, 0:D]]
            summed = work[7][:, D:2 * D]
            u_sums = ps[:, 2:4, :].rearrange("p b (h v) -> p (b h) v", v=P)

            def keep_causal(t):
                dve.wait_ge(a_done, t + 1)
                for h in range(H):
                    ins = nc.vector.copy_predicated(tokens(tT)[:, t, h * P:(h + 1) * P], chunk_mask[:].bitcast(U32),
                                                    ps[:, 2 * t + h // 4, (h % 4) * P:(h % 4) * P + P])
                ins.then_inc(at_evac, 1)

            for c in range(AT_WO):
                if c == 14:
                    keep_causal(1)
                if c < AT_WO - 1:
                    split_lo(dve, c + SPLIT_SLOTS)
                g = c // 2
                half = slice(1024 * (g % 2), 1024 * (g % 2) + 1024)
                if c in (1, 3):
                    features_out(c, g, g, zT)
                    dve.wait_ge(group_free[g % 2], g // 2 + 1)
                    nc.vector.tensor_copy(soft[:, 0, 0:1], zT[:, 0:1]).then_inc(scaled, 1)
                if c == 4:
                    dve.wait_ge(ln_ready, 1)
                    link(nc.vector.scalar_tensor_tensor(zT[:], zT[:], 0.0, tT[:], ALU.min, ALU.add))
                if c in (4, 5):
                    for h in range(4 * (c - 4), 4 * (c - 4) + 4):
                        ins = nc.vector.tensor_tensor_scan(heads(tT)[:, h, :], scan_keep[:].rearrange("p n c -> p (n c)"),
                                                           heads(zT)[:, h, :], 0.0, ALU.mult, ALU.add)
                if c == 6:
                    link(nc.vector.memset(alpha[:, :, NCH - 1:NCH], 0.0))
                    by_chunk = heads(tT).rearrange("p h (n c) -> p h n c", c=CH)
                    nc.vector.tensor_copy(b_ref[:], by_chunk[:, :, :, CH // 2 - 1])
                    link(nc.vector.tensor_copy(b_last[:], by_chunk[:, :, :, CH - 1]))
                    link(nc.vector.tensor_tensor(alpha[:, :, 0:NCH - 1], b_ref[:, :, 1:NCH], b_ref[:, :, 0:NCH - 1], ALU.subtract))
                    nc.vector.tensor_tensor(alpha[:, :, 0:NCH - 1], alpha[:, :, 0:NCH - 1], b_last[:, :, 0:NCH - 1], ALU.add)
                    ref = b_ref[:].rearrange("p h n -> p (h n)").unsqueeze(2).broadcast_to([P, H * NCH, CH])
                    nc.vector.tensor_tensor(chunks(zT), chunks(tT), ref, ALU.subtract).then_inc(arg_ready, 1)
                if c == 8:
                    dve.wait_ge(e2_ready, 1)
                    nc.vector.tensor_tensor(kT[:], kT[:], zT[:], ALU.mult).then_inc(k_ready, 1)
                if c in (9, 11):
                    features_out(c, g, g % 2, qT)
                    dve.wait_ge(group_free[g % 2], g // 2 + 1)
                    nc.vector.tensor_copy(soft[:, 0, 0:1], qT[:, 0:1]).then_inc(scaled, 1)
                if c in (10, 12):
                    i = (c - 10) // 2
                    dve.wait_ge(q_silu, i + 1)
                    part = slice(1024 * i, 1024 * i + 1024)
                    nc.vector.tensor_tensor(qT[:, part], qT[:, part], tT[:, part], ALU.mult).then_inc(q_ready, 1)
                if c == 11:
                    dve.wait_ge(alpha_ready, 1)
                    dve.wait_ge(u_done, 1)
                    nc.vector.tensor_tensor(by_head(states[0]), u_sums, carry(0), ALU.mult).then_inc(s_ready, 1)
                if c in (12, 13):
                    n = c - 11
                    dve.wait_ge(s_ready, n)
                    dve.wait_ge(u_done, n + 1)
                    nc.vector.tensor_tensor(by_head(summed), by_head(states[n - 1]), u_sums, ALU.add).then_inc(u_free, 1)
                    dve.wait_ge(u_free, n)
                    nc.vector.tensor_tensor(by_head(states[n]), by_head(summed), carry(n), ALU.mult).then_inc(s_ready, 1)
                if c == 13:
                    dve.wait_ge(scores_clear, 1)
                    keep_causal(0)

            for t in range(TT):
                dve.wait_ge(o_sq, t + 1)
                link(nc.vector.tensor_reduce(head_rstd[:, t, :], by_head(tokens(zT)[:, t, :]), AX_X, ALU.add))
                nc.vector.tensor_scalar(head_ms[:, t, :], head_rstd[:, t, :], 1.0 / P, EPS, ALU.mult, ALU.add).then_inc(o_ms, 1)
            for t in range(TT):
                dve.wait_ge(o_std, t + 1)
                ins = nc.vector.reciprocal(head_rstd[:, t, :], head_std[:, t, :])
            link(ins)
            for b in range(2):
                dve.wait_ge(group_free[b], 4)
                for t in range(TT):
                    for i in range(4):
                        h = 4 * b + i
                        cols = slice(h * P, (h + 1) * P)
                        ins = nc.vector.scalar_tensor_tensor(tokens(kT)[:, t, cols], ps[:, 2 * t + b, i * P:(i + 1) * P],
                                                             head_rstd[:, t, h:h + 1], tokens(g_tm)[:, t, cols], ALU.mult, ALU.mult)
                    ins.then_inc(on_ready, 1)

            def outputs_lo(b):
                for t in range(TT):
                    dve.wait_ge(ot_hi, 2 * b + t + 1)
                    for i in range(4):
                        k = 4 * b + i
                        ins = nc.vector.scalar_tensor_tensor(h_lo[:, k, t * P:(t + 1) * P], ps[:, 4 + 2 * b + t, i * P:(i + 1) * P],
                                                             gains[:, GAIN_OUT + k:GAIN_OUT + k + 1],
                                                             h_hi[:, k, t * P:(t + 1) * P].bitcast(F32), ALU.mult, ALU.subtract)
                    ins.then_inc(ot_lo, 1)

            outputs_lo(0)
            outputs_lo(1)
            split_lo(dve, AT_WO - 1 + SPLIT_SLOTS)
            for c in range(AT_WO, AT_FFN):
                if c == AT_FFN - 2:
                    norm_lo(GAIN_FFN0, 4, 0)
                if c < AT_FFN - 1:
                    split_lo(dve, c + SPLIT_SLOTS)
                if (c - AT_WO) % 2 == 1:
                    i = (c - AT_WO) // 2
                    add_group(c, GR_WO + i, i)
            norm_lo(GAIN_FFN0, 4, 1)
            split_lo(dve, AT_FFN - 1 + SPLIT_SLOTS)

            norm_row(1)
            for n, (kind, j, m) in enumerate(ffn_panels):
                last_g = kind == "G" and j == FG - 1 and m == 1
                if n < len(ffn_panels) - 2 and not last_g:
                    split_lo(dve, AT_FFN + n + SPLIT_SLOTS)
                if kind == "G" and m == 1:
                    g = GR_FFN + j
                    b = pair(g)
                    if j >= 2:
                        dve.wait_ge(alo_ready, j - 1)
                    dve.wait_ge(panel_used, AT_FFN + n + 1)
                    gate, a = gu[:, j % 2, 0], gu[:, j % 2, 0].rearrange("p f s -> p (f s)")
                    nc.vector.tensor_tensor(gate, ps[:, b:b + 2, 0:S], rms_row[:].unsqueeze(1).broadcast_to([P, 2, S]),
                                            ALU.mult).then_inc(scaled, 1)
                    dve.wait_ge(silu_ready, j + 1)
                    nc.vector.tensor_tensor(gate, gate, ps[:, b:b + 2, S:2 * S], ALU.mult).then_inc(act_ready, 1)
                    dve.wait_ge(ahi_ready, j + 1)
                    nc.vector.tensor_tensor(a_lo[:, j % 2, :], a, a_hi[:, j % 2, :].bitcast(F32), ALU.subtract).then_inc(alo_ready, 1)
                if last_g:
                    split_lo(dve, AT_FFN + n + SPLIT_SLOTS)
            for i in range(2):
                if i == 0:
                    dve.wait_ge(down_half, 1)
                else:
                    dve.wait_ge(panel_used, AT_Q)
                for t in range(TT):
                    xs = x_res[:, t, 512 * i:512 * i + 512]
                    nc.vector.scalar_tensor_tensor(xs, ps[:, 2 * i + t, :], rstd[:, 1, t:t + 1], xs, ALU.mult, ALU.add).then_inc(x_added, 1)
                if i == 0:
                    norm_lo(GAIN_ATTN1, 8, 0, q_hi, q_lo)
            split_lo(dve, AT_Q - 2 + SPLIT_SLOTS)
            norm_mean(2)
            norm_lo(GAIN_ATTN1, 8, 1, q_hi, q_lo)
            split_lo(dve, AT_Q - 1 + SPLIT_SLOTS)

            norm_row(2, pair(GR_Q + 1), ms=False)

            def biased(h):
                p = probs[h % 4]
                dve.wait_ge(sc_done, h + 1)
                if h >= 4:
                    dve.wait_ge(pt_done, h - 3)
                for t, part in enumerate((slice(0, P), slice(P, 3 * P))):
                    ins = nc.vector.tensor_tensor_reduce(p[:, part], ps[:, h % 2, part], bias[h][:, part], 1.0, -3e38,
                                                         ALU.add, ALU.max, soft[:, h, t:t + 1])
                link(ins)
                nc.vector.tensor_scalar(soft[:, h, 2:4], soft[:, h, 0:2], -SCALE, None, ALU.mult).then_inc(max_ready, 1)

            def normalised(h):
                p = probs[h % 4]
                dve.wait_ge(exp_ready, h + 1)
                link(nc.vector.reciprocal(soft[:, h, 6:8], soft[:, h, 4:6]))
                nc.vector.tensor_scalar(p[:, 0:P], p[:, 0:P], soft[:, h, 6:7], None, ALU.mult)
                nc.vector.tensor_scalar(p[:, P:3 * P], p[:, P:3 * P], soft[:, h, 7:8], None, ALU.mult).then_inc(p_ready, 1)

            dve.wait_ge(bias_ready, 1)
            for c in range(AT_Q, AT_WO2):
                if AT_V - 1 <= c < AT_WO2 - 1:
                    h = 2 * (c - AT_V) + 2
                    for i in (h, h + 1):
                        biased(i)
                    for i in (h, h + 1):
                        normalised(i)
                if c < AT_WO2 - 1:
                    split_lo(dve, c + SPLIT_SLOTS)
                g = GR_Q + (c - AT_Q) // 2
                if (c - AT_Q) % 2 == 1 and c < AT_V:
                    features_out(c, g, (g - GR_Q) % 2, qT if c < AT_KV else kT)
                if c in (AT_Q, AT_Q + 1):
                    norm_lo(GAIN_KV, 12, c - AT_Q)
            for h in range(H):
                dve.wait_ge(ov_hi, h + 1)
                nc.vector.tensor_tensor(h_lo[:, h, :], ps[:, 4 + h % 4, 0:S], h_hi[:, h, :].bitcast(F32),
                                        ALU.subtract).then_inc(ov_lo, 1)
            split_lo(dve, AT_WO2 - 1 + SPLIT_SLOTS)
            for c in range(AT_WO2, MOE0):
                if c < MOE0 - 1:
                    split_lo(dve, c + SPLIT_SLOTS)
                if (c - AT_WO2) % 2 == 1:
                    i = (c - AT_WO2) // 2
                    add_group(c, GR_WO2 + i, i)
            dve.wait_ge(group_free[1], (GR_WO2 + 1) // 2 + 1)
            for t in range(TT):
                ins = nc.vector.tensor_tensor_reduce(junk[:], x_res[:, t, :], x_res[:, t, :], 1.0, 0.0, ALU.mult, ALU.add,
                                                     sumsq[:, 3, t:t + 1])
                link(ins)
            nc.vector.tensor_scalar(mean_sq[:, 3, :], sumsq[:, 3, :], 1.0 / D, EPS, ALU.mult, ALU.add).then_inc(ms_ready, 1)

            r = route
            dve.wait_ge(logits_done, 1)
            link(nc.vector.tensor_copy(r[:, :, 0, :], ps[:, 4:4 + TT, 0:E]))
            for t in range(TT):
                ins = nc.vector.max(r[:, t, 1, :], r[:, t, 0, :])
            link(ins)
            for t in range(TT):
                ins = nc.vector.max_index(route_u[:, t, :], r[:, t, 1, :], r[:, t, 0, :])
            link(ins)
            link(nc.vector.tensor_copy(r[:, :, 4, :], route_u[:]))
            for t in range(TT):
                for i in range(2):
                    ins = nc.vector.tensor_scalar(r[:, t, 5 + i, :], expert_id[:], r[:, t, 4, i:i + 1], None, ALU.is_equal)
            link(ins)
            nc.vector.tensor_tensor(r[:, :, 7, :], r[:, :, 5, :], r[:, :, 6, :], ALU.add).then_inc(picked, 1)
            norm_scale(3, ms=False)
            dve.wait_ge(late_loaded, 32)
            for t in range(TT):
                nc.vector.scalar_tensor_tensor(tokens(xn)[:, t, :], x_res[:, t, :], rstd[:, 3, t:t + 1], moe_gain,
                                               ALU.mult, ALU.mult).then_inc(h_ready, 1)
            dve.wait_ge(ranks_done, 1)
            rank_ps = ps[:, 5, 0:TT * E].rearrange("p (t e) -> p t e", t=TT)
            link(nc.vector.scalar_tensor_tensor(r[:, :, 10, :], rank_ps, 1.0, r[:, :, 7, :], ALU.add, ALU.mult))
            link(nc.vector.tensor_scalar(r[:, :, 10, :], r[:, :, 10, :], -1.0, None, ALU.add))
            for t in range(TT):
                ins = nc.vector.tensor_scalar(sel[:, t, :], slot_id[:], r[:, t, 10, 0:1], None, ALU.is_equal)
            ins.then_inc(m_sel, 1)

            for t in range(TT):
                dve.wait_ge(xn_rounded, t + 1)
                cols = slice(t * D, (t + 1) * D)
                nc.vector.tensor_tensor(xn_lo[:, cols], xn[:, cols], xn_hi[:, cols].bitcast(F32), ALU.subtract).then_inc(xn_split, 1)
            split_lo(dve, MOE0 - 1 + SPLIT_SLOTS)

            def gather_lo(passes):
                for b in range(2):
                    dve.wait_ge(m_ghi, 2 * passes + b + 1)
                    nc.vector.tensor_tensor(h_lo[:, 4 * b:4 * b + 4, 0:P], ps[:, (7, 2)[b], :].rearrange("p (k s) -> p k s", k=4),
                                            h_hi[:, 4 * b:4 * b + 4, 0:P].bitcast(F32), ALU.subtract).then_inc(m_glo, 1)

            gather_lo(0)
            link(nc.vector.tensor_tensor(r[:, :, 2, 1:2], r[:, :, 1, 1:2], r[:, :, 1, 0:1], ALU.subtract))
            nc.vector.tensor_tensor(r[:, :, 2, 0:1], r[:, :, 2, 1:2], rstd[:, 3, :].unsqueeze(2), ALU.mult).then_inc(gap_ready, 1)

            def gate_tables():
                nc.vector.memset(pass_rank[:], -1.0)
                link(nc.vector.memset(pass_gate[:], 0.0))
                dve.wait_ge(gate_exp, 1)
                link(nc.vector.tensor_scalar(r[:, :, 2, 1:2], r[:, :, 3, 0:1], 1.0, None, ALU.add))
                link(nc.vector.reciprocal(r[:, :, 2, 2:3], r[:, :, 2, 1:2]))
                link(nc.vector.tensor_tensor(r[:, :, 2, 3:4], r[:, :, 2, 2:3], r[:, :, 3, 0:1], ALU.mult))
                for t in range(TT):
                    link(nc.vector.tensor_scalar(r[:, t, 8, :], r[:, t, 6, :], r[:, t, 2, 3:4], None, ALU.mult))
                    ins = nc.vector.scalar_tensor_tensor(r[:, t, 9, :], r[:, t, 5, :], r[:, t, 2, 2:3], r[:, t, 8, :], ALU.mult, ALU.add)
                link(ins)
                nc.vector.tensor_copy(pass_rank[:, :, 1:E], r[:, :, 10, 0:E - 1])
                nc.vector.tensor_copy(pass_gate[:, :, 1:E], r[:, :, 9, 0:E - 1])
                nc.vector.tensor_scalar(r[:, :, 11, 0:1], r[:, :, 10, E - 1:E], 1.0, None, ALU.add)
                nc.vector.tensor_scalar(over[:, 0, :], ps[:, 5, TT * E:TT * E + E], float(P), None, ALU.is_gt)
                link(nc.vector.memset(over[:, 7, :], 1.0))
                link(nc.vector.tensor_tensor_scan(over[:, 1, :], over[:, 7, :], over[:, 0, :], 0.0, ALU.mult, ALU.add))

            def extra_table(k):
                link(nc.vector.tensor_scalar(over[:, 2, :], over[:, 1, :], float(k + 1), None, ALU.is_equal))
                link(nc.vector.tensor_tensor(over[:, 2, :], over[:, 2, :], over[:, 0, :], ALU.mult))
                link(nc.vector.tensor_tensor(over[:, 3, :], over[:, 2, :], expert_id[:], ALU.mult))
                if k < EXTRA:
                    nc.vector.tensor_reduce(info_f[:, k + 1:k + 2], over[:, 3, :], AX_X, ALU.add)
                picks = over[:, 2, :].unsqueeze(1).broadcast_to([P, TT, E])
                nc.vector.tensor_tensor(picked_gate[:], r[:, :, 9, :], picks, ALU.mult)
                link(nc.vector.scalar_tensor_tensor(picked_rank[:], r[:, :, 10, :], 1.0 - P, picks, ALU.add, ALU.mult))
                gate, rank = pass_gate[:, :, E + k:E + k + 1], pass_rank[:, :, E + k:E + k + 1]
                nc.vector.tensor_scalar(over[:, 4, 0:1], over[:, 1, E - 1:E], float(k), None, ALU.is_equal)
                link(nc.vector.tensor_reduce(gate, picked_gate[:], AX_X, ALU.add))
                nc.vector.scalar_tensor_tensor(gate, r[:, :, 9, E - 1:E], over[:, 4, 0:1], gate, ALU.mult, ALU.add)
                link(nc.vector.tensor_reduce(over[:, 6, 0:TT], picked_rank[:], AX_X, ALU.add))
                link(nc.vector.tensor_scalar(rank, over[:, 6, 0:TT].unsqueeze(2), -1.0, None, ALU.add))
                link(nc.vector.scalar_tensor_tensor(rank, r[:, :, 11, 0:1], over[:, 4, 0:1], rank, ALU.mult, ALU.add))

            def tables_out():
                link(nc.vector.tensor_copy(info_f[:, 0:1], over[:, 1, E - 1:E]))
                nc.vector.tensor_copy(info[:], info_f[:]).then_inc(info_ready, 1)
                dve.wait_ge(info_ready, 1)

            def add_back(p, q, bank=7):
                t, i = q // 2, q % 2
                dve.wait_ge(m_scat, p * 4 + (q - 3))
                xs = x_res[:, t, 512 * i:512 * i + 512]
                nc.vector.scalar_tensor_tensor(xs, ps[:, bank, :], pass_gate[:, t, bass.ds(p, 1)], xs,
                                               ALU.mult, ALU.add).then_inc(m_add, 1)

            def expert(p, last=False):
                def turned_lo(j):
                    dve.wait_ge(m_ahi, p * EG + j + 1)
                    nc.vector.tensor_tensor(a_lo[:, j % 2, :], ps[:, 6, :], a_hi[:, j % 2, :].bitcast(F32),
                                            ALU.subtract).then_inc(m_alo, 1)

                for c, (kind, j, m) in enumerate(moe_panels):
                    if kind == "D" and j == EG - 2 and m == 0:
                        turned_lo(EG - 1)
                    if kind == "D" and j == EG - 1 and m == 0 and not last:
                        gather_lo(p + 1)
                    if kind == "G" and m == 3:
                        dve.wait_ge(m_silu, p * EG + j + 1)
                        s = junk[:, 512 * (j % 2):512 * (j % 2) + 512]
                        nc.vector.tensor_tensor(s, s, ps[:, 2 * (j % 2) + 1, :], ALU.mult).then_inc(m_act, 1)
                    split_lo(dve, MOE0 + c + SPLIT_SLOTS, p, last)
                    first = isinstance(p, int)
                    if first:
                        if c == 0:
                            gate_tables()
                        if c % 4 == 2 and c // 4 <= EXTRA:
                            extra_table(c // 4)
                        if c == 4 * EXTRA + 6:
                            tables_out()
                    if kind == "G" and m == 1:
                        if j >= 1:
                            turned_lo(j - 1)
                        if j < 2 and not first:
                            add_back(p, 2 * j)
                    if kind == "G" and m == 3:
                        if j < 2 and not first:
                            add_back(p, 2 * j + 1)
                        if j == 3 and not last:
                            dve.wait_ge(m_selturn, p + 1)
                            for t in range(TT):
                                ins = nc.vector.tensor_scalar(sel[:, t, :], slot_id[:], pass_rank[:, t, bass.ds(p + 2, 1)], None,
                                                              ALU.is_equal)
                            ins.then_inc(m_sel, 1)

            expert(0)
            with dve.Fori(1, E - 1) as p:
                expert(p)
            extra = dve.value_load(info[0:1, 0:1], min_val=0, max_val=EXTRA)
            with dve.If(extra > 0):
                with dve.Fori(0, extra) as i:
                    expert(i + (E - 1))
            expert(extra + (E - 1), last=True)
            for q in range(4):
                add_back(extra + E, q, bank=q)
            dve.wait_ge(final_loaded, 16)
            for t in range(TT):
                dve.wait_ge(sq_done, TT * 3 + t + 1)
                nc.vector.tensor_scalar(mean_sq[:, 4, t:t + 1], sumsq[:, 4, t:t + 1], 1.0 / D, EPS, ALU.mult, ALU.add).then_inc(ms_ready, 1)
                dve.wait_ge(std_ready, 5 + t)
                link(nc.vector.reciprocal(rstd[:, 4, t:t + 1], std[:, 4, t:t + 1]))
                nc.vector.scalar_tensor_tensor(tokens(xn)[:, t, :], x_res[:, t, :], rstd[:, 4, t:t + 1], final_gain,
                                               ALU.mult, ALU.mult).then_inc(out_ready, 1)

        @block.tensor
        def _(pe):
            def product(out_ap, lhs, rhs, start, stop, share=False):
                (lh, ll), (rh, rl) = lhs, rhs
                nc.tensor.matmul(out_ap, lh, rh, start=start, stop=False, skip_group_check=share)
                nc.tensor.matmul(out_ap, lh, rl, start=False, stop=False, skip_group_check=share)
                return nc.tensor.matmul(out_ap, ll, rh, start=False, stop=stop, skip_group_check=share)

            def weights(c, a, n):
                s = c % SPLIT_SLOTS
                return w_hi[:, s, a:a + n], w_lo[:, s, a:a + n]

            def acts(k, t0, n):
                return h_hi[:, k, t0:t0 + n], h_lo[:, k, t0:t0 + n]

            def feature_panel(c, g, kh, middle=None, ops=(h_hi, h_lo), at=1):
                pe.wait_ge(lo_ready, c + 1)
                for k in range(4):
                    for f in range(4):
                        o = ps[:, pair(g) + f // 2, (f % 2) * S:(f % 2) * S + S]
                        ins = product(o, weights(c, k * 512 + f * P, P), tuple(a[:, 4 * kh + k, :] for a in ops),
                                      start=(kh == 0 and k == 0 and f % 2 == 0), stop=(kh == 1 and k == 3), share=True)
                    if k == at and middle:
                        middle()
                ins.then_inc(panel_used, 1)

            def token_panel(c, g, kh, middle=None):
                pe.wait_ge(lo_ready, c + 1)
                for k in range(4):
                    for t in range(TT):
                        ins = product(ps[:, pair(g) + t, :], acts(4 * kh + k, t * P, P), weights(c, k * 512, 512),
                                      start=(kh == 0 and k == 0), stop=(kh == 1 and k == 3))
                    if k == 1 and middle:
                        middle()
                ins.then_inc(panel_used, 1)

            def keep_clock(n, w, x):
                for _ in range(n):
                    nc.tensor.matmul(ps[:, 6, 0:x.shape[1]], w, x, start=True, stop=True)

            def group_begins(g):
                if g >= 2:
                    pe.wait_ge(group_free[g % 2], g // 2)

            def turn_tokens(half):
                for b in (2 * half, 2 * half + 1):
                    for i in range(2):
                        for t in range(TT):
                            k = 2 * b + i
                            ins = nc.tensor.transpose(ps[:, b, i * S + t * P:i * S + (t + 1) * P],
                                                      x_res[:, t, k * P:(k + 1) * P], ident[:])
                    ins.then_inc(tr_done, 1)

            def spread_rms(n, bank=0):
                pe.wait_ge(diag_ready, n + 1)
                for t in range(TT):
                    ins = nc.tensor.matmul(ps[:, bank, t * P:(t + 1) * P], ones[:], diag[:, t, :], start=True, stop=True)
                ins.then_inc(row_done, 1)

            pe.wait_ge(consts, 2)
            keep_clock(WARM[0], ident[:], ident[:])
            pe.wait_ge(x_loaded, 16)
            turn_tokens(0)
            pe.wait_ge(attn_gains_loaded, 16)
            nc.tensor.transpose(ps[:, 7, 0:2 * KT], gain_rows[0:2 * KT, :], ident[0:2 * KT, 0:2 * KT]).then_inc(gains_turned, 1)
            turn_tokens(1)
            keep_clock(WARM[1], ident[:], ident[:])
            pe.wait_ge(gains_ready, 1)
            pe.wait_ge(gains_loaded, 48)
            nc.tensor.transpose(ps[:, 7, 0:6 * KT], gain_rows[:], ident[0:6 * KT, 0:6 * KT]).then_inc(gains_turned, 1)

            def qh(h, a, n):
                return heads(qT)[:, h, a:a + n]

            def kh_(h, a, n):
                return heads(kT)[:, h, a:a + n]

            def vh(t, h, a=0, n=P):
                return tokens(v_tm)[a:a + n, t, h * P:(h + 1) * P]

            def turn_k(t):
                for b in range(2):
                    if t:
                        pe.wait_ge(kt_evac, b + 1)
                    for h in range(4 * b, 4 * b + 4):
                        ins = nc.tensor.transpose(ps[:, b, (h % 4) * P:(h % 4) * P + P], kh_(h, t * P, P), ident[:])
                    ins.then_inc(kt_done, 1)

            def scores(t):
                for h in range(H):
                    ins = nc.tensor.matmul(ps[:, 2 * t + h // 4, (h % 4) * P:(h % 4) * P + P], kh_(h, t * P, P), qh(h, t * P, P),
                                           start=True, stop=True)
                ins.then_inc(a_done, 1)

            def sums(n):
                t, a = n // 2, CH * (n % 2)
                if n:
                    if n == 1:
                        pe.wait_ge(s_ready, 1)
                    else:
                        pe.wait_ge(u_free, n - 1)
                pe.wait_ge(kt_evac, 2 * t + 2)
                for h in range(H):
                    ins = nc.tensor.matmul(ps[:, 2 + h // 4, (h % 4) * P:(h % 4) * P + P],
                                           tokens(zT)[a:a + CH, t, h * P:(h + 1) * P], vh(t, h, a, CH), start=True, stop=True)
                ins.then_inc(u_done, 1)

            def outputs(t):
                pe.wait_ge(at_evac, t + 1)
                pe.wait_ge(s_ready, 1 if t == 0 else 3)
                states = [work[6][:, 0:D], work[6][:, D:2 * D], work[7][:, 0:D]]
                for h in range(H):
                    bank, cols = 2 * t + h // 4, slice((h % 4) * P, (h % 4) * P + P)
                    ins = nc.tensor.matmul(ps[:, bank, cols], tokens(tT)[:, t, h * P:(h + 1) * P], vh(t, h),
                                           start=(h % 4 == 0), stop=True, skip_group_check=True)
                    for half in range(2):
                        n = 2 * t + half
                        if n:
                            ins = nc.tensor.matmul(ps[CH * half:CH * half + CH, bank, cols],
                                                   qh(h, n * CH, CH), states[n - 1][:, h * P:(h + 1) * P],
                                                   start=False, stop=True, skip_group_check=True)
                ins.then_inc(o_done, 1)

            for g in range(8):
                group_begins(g)
                for kh in range(2):
                    c = 2 * g + kh
                    if g == 0:
                        pe.wait_ge(lo_done, 2 * kh + 2)
                    (token_panel if g in (2, 3, 6, 7) else feature_panel)(c, g, kh)
                    if c == 0:
                        pe.wait_ge(lo_done, 4)
                        spread_rms(0)
                    if c == 1:
                        pe.wait_ge(gains_ready, 2)
                        pe.wait_ge(consts, CONSTS)
                    if c == 10:
                        pe.wait_ge(k_ready, 1)
                        pe.wait_ge(row_ready, 1)
                        turn_k(0)
                    if c == 11:
                        pe.wait_ge(group_free[1], 2)
                        sums(0)
                        turn_k(1)
                    if c == 12:
                        sums(1)
                    if c == 13:
                        sums(2)
                        pe.wait_ge(q_ready, 2)
                        pe.wait_ge(kt_evac, 4)
                        scores(0)
                    if c == 14:
                        pe.wait_ge(u_free, 2)
                        scores(1)
                        outputs(0)
                        outputs(1)

            def turn_outputs(b):
                pe.wait_ge(group_free[b], 4)
                for t in range(TT):
                    pe.wait_ge(on_ready, 2 * b + t + 1)
                    for i in range(4):
                        k = 4 * b + i
                        ins = nc.tensor.transpose(ps[:, 4 + 2 * b + t, i * P:(i + 1) * P], tokens(kT)[:, t, k * P:(k + 1) * P], ident[:])
                    ins.then_inc(ot_done, 1)

            def next_half(i):
                pe.wait_ge(group_free[i], (GR_WO + i) // 2 + 1)
                turn_tokens(i)

            turn_outputs(0)
            turn_outputs(1)
            for i in range(2):
                for kh in range(2):
                    if i == 0:
                        pe.wait_ge(ot_lo, 2 * kh + 2)
                    token_panel(AT_WO + 2 * i + kh, GR_WO + i, kh)
                    if i == 1 and kh == 0:
                        next_half(0)

            for n, (kind, j, m) in enumerate(ffn_panels):
                c = AT_FFN + n
                if kind == "G":
                    if m == 0 and j < 2:
                        group_begins(GR_FFN + j)
                    elif m == 0:
                        pe.wait_ge(act_ready, j - 1)
                    if j == 0:
                        pe.wait_ge(lo_done, 4 + 2 * m + 2)
                    pe.wait_ge(lo_ready, c + 1)
                    for k in range(4):
                        for f in range(2):
                            for u in range(2):
                                o = ps[:, pair(GR_FFN + j) + f, u * S:(u + 1) * S]
                                ins = product(o, weights(c, k * 512 + u * 256 + f * P, P), acts(4 * m + k, 0, S),
                                              start=(m == 0 and k == 0 and u == 0), stop=(m == 1 and k == 3), share=True)
                        if (j, m, k) == (0, 0, 1):
                            next_half(1)
                    ins.then_inc(panel_used, 1)
                    if j == 0 and m == 1:
                        spread_rms(1)
                else:
                    pe.wait_ge(alo_ready, j + 1)
                    pe.wait_ge(lo_ready, c + 1)
                    if j == 0:
                        pe.wait_ge(row_ready, 2)
                    for i in range(2):
                        for k in range(2):
                            for t in range(TT):
                                at = k * S + t * P
                                ins = product(ps[:, 2 * i + t, :], (a_hi[:, j % 2, at:at + P], a_lo[:, j % 2, at:at + P]),
                                              weights(c, k * D + i * 512, 512),
                                              start=(j == 0 and k == 0), stop=(j == FG - 1 and k == 1))
                            if j == FG - 1 and (i, k) == (1, 0):
                                pe.wait_ge(x_added, 2)
                                turn_tokens(0)
                        if j == FG - 1 and i == 0:
                            ins.then_inc(down_half, 1)
                    ins.then_inc(panel_used, 1)

            def attn_scores(h):
                if h >= 2:
                    pe.wait_ge(max_ready, h - 1)
                nc.tensor.matmul(ps[:, h % 2, 0:P], qh(h, 0, P), kh_(h, 0, P), start=True, stop=True)
                nc.tensor.matmul(ps[:, h % 2, P:3 * P], qh(h, P, P), kh_(h, 0, S), start=True, stop=True).then_inc(sc_done, 1)

            def turn_p(h):
                pe.wait_ge(p_ready, h + 1)
                if h >= 2:
                    pe.wait_ge(pt_evac, h - 1)
                for at in range(0, 3 * P, P):
                    ins = nc.tensor.transpose(ps[:, 2 + h % 2, at:at + P], probs[h % 4][:, at:at + P], ident[:])
                ins.then_inc(pt_done, 1)

            def second_half():
                pe.wait_ge(x_added, 4)
                turn_tokens(1)

            for g in range(GR_Q, GR_WO2):
                group_begins(g)
                if g == GR_Q + 1:
                    pe.wait_ge(row_ready, 3)
                for kh in range(2):
                    c = AT_Q + 2 * (g - GR_Q) + kh
                    if g in (GR_Q, GR_Q + 2):
                        pe.wait_ge(lo_done, (8 if g == GR_Q else 12) + 2 * kh + 2)
                    if g < GR_Q + 2:
                        middle = {AT_Q: second_half, AT_Q + 1: lambda: spread_rms(2, pair(GR_Q + 1))}.get(c)
                        feature_panel(c, g, kh, middle, (q_hi, q_lo), 1 if c == AT_Q else 2)
                    elif c < AT_V:
                        feature_panel(c, g, kh)
                    else:
                        token_panel(c, g, kh)
                    if c >= AT_V:
                        turn_p(2 * (c - AT_V))
                        turn_p(2 * (c - AT_V) + 1)
                    if AT_V - 2 <= c < AT_WO2 - 2:
                        h = 2 * (c - AT_V) + 4
                        if h == 0:
                            pe.wait_ge(group_free[0], GR_Q // 2 + 2)
                            pe.wait_ge(group_free[1], GR_Q // 2 + 1)
                        if h == 4:
                            pe.wait_ge(group_free[1], GR_Q // 2 + 2)
                        attn_scores(h)
                        attn_scores(h + 1)
            pe.wait_ge(group_free[0], (GR_WO2 + 1) // 2)
            pe.wait_ge(group_free[1], GR_WO2 // 2)
            for h in range(H):
                pe.wait_ge(pt_evac, h + 1)
                if h >= 4:
                    pe.wait_ge(ov_lo, h - 3)
                nc.tensor.matmul(ps[:, 4 + h % 4, 0:S], vh(0, h), turned_p[h][:, 0:S], start=True, stop=False, skip_group_check=True)
                nc.tensor.matmul(ps[:, 4 + h % 4, P:S], vh(1, h), turned_p[h][:, S:3 * P], start=False, stop=True,
                                 skip_group_check=True).then_inc(ov_done, 1)
            def logits(half):
                if half == 0:
                    pe.wait_ge(late_loaded, 32)
                pe.wait_ge(hf_ready, 2 * half + 2)
                for t in range(TT):
                    for k in range(4 * half, 4 * half + 4):
                        ins = nc.tensor.matmul(ps[:, 4 + t, 0:E], heads(router_x)[:, k, t * P:(t + 1) * P], router[:, k, :],
                                               start=(k == 0), stop=(k == KT - 1))
                if half == 1:
                    ins.then_inc(logits_done, 1)

            for i in range(2):
                for kh in range(2):
                    middle = (lambda: logits(0)) if (i, kh) == (1, 1) else None
                    if i == 0:
                        pe.wait_ge(ov_lo, 6 + 2 * kh)
                    token_panel(AT_WO2 + 2 * i + kh, GR_WO2 + i, kh, middle)
                    if i == 1 and kh == 0:
                        pe.wait_ge(group_free[GR_WO2 % 2], GR_WO2 // 2 + 1)
                        turn_tokens(0)
            pe.wait_ge(group_free[(GR_WO2 + 1) % 2], (GR_WO2 + 1) // 2 + 1)
            turn_tokens(1)

            idle = (h_hi[:, 0, 0:P], w_hi[:, MOE0 % SPLIT_SLOTS, 0:512])
            keep_clock(WARM[2], *idle)
            logits(1)
            keep_clock(WARM[3], *idle)
            pe.wait_ge(picked, 1)
            nc.tensor.matmul(ps[:, 5, 0:E], earlier[:], route[:, 0, 7, :], start=True, stop=True)
            nc.tensor.matmul(ps[:, 5, E:2 * E], ones[:], route[:, 0, 7, :], start=True, stop=False)
            nc.tensor.matmul(ps[:, 5, E:2 * E], earlier[:], route[:, 1, 7, :], start=False, stop=True)
            nc.tensor.matmul(ps[:, 5, 2 * E:3 * E], ones[:], route[:, 0, 7, :], start=True, stop=False)
            nc.tensor.matmul(ps[:, 5, 2 * E:3 * E], ones[:], route[:, 1, 7, :], start=False, stop=True).then_inc(ranks_done, 1)
            keep_clock(WARM[4], *idle)

            def gather(passes):
                pe.wait_ge(m_sel, passes + 1)
                for part, xs, ready in ((0, xn_hi, xn_rounded), (1, xn_lo, xn_split)):
                    pe.wait_ge(ready, TT)
                    for b in range(2):
                        for i in range(4):
                            for t in range(TT):
                                at = t * D + (4 * b + i) * P
                                ins = nc.tensor.matmul(ps[:, (7, 2)[b], i * P:(i + 1) * P], xs[:, at:at + P], sel[:, t, :],
                                                       start=(part == 0 and i == 0 and t == 0), stop=(part == 1 and t == TT - 1),
                                                       skip_group_check=True)
                        if part == 1:
                            ins.then_inc(m_gath, 1)

            def scatter(p, q, bank=7):
                t, i = q // 2, q % 2
                pe.wait_ge(m_out, p)
                if q and bank == 7:
                    pe.wait_ge(m_add, p * 4 + (q - 4))
                nc.tensor.matmul(ps[:, bank, :], sel_T[:, t * P:(t + 1) * P], work[1][:, 512 * i:512 * i + 512],
                                 start=True, stop=True).then_inc(m_scat, 1)

            gather(0)

            def expert(p, last=False):
                def turn(j):
                    pe.wait_ge(m_act, p * EG + j + 1)
                    if j:
                        pe.wait_ge(m_alo, p * EG + j)
                    for i in range(4):
                        ins = nc.tensor.transpose(ps[:, 6, i * P:(i + 1) * P],
                                                  junk[:, 512 * (j % 2) + i * P:512 * (j % 2) + (i + 1) * P], ident[:])
                    ins.then_inc(m_turn, 1)

                pe.wait_ge(m_glo, p * 2 + 2)
                for c, (kind, j, m) in enumerate(moe_panels):
                    first = isinstance(p, int)
                    if kind == "D" and j == EG - 2 and m == 1:
                        turn(EG - 1)
                    if kind == "D" and j == EG - 1 and m == 0 and not last:
                        pe.wait_ge(m_selT, p + 1)
                        gather(p + 1)
                    if kind == "G" and m == 0 and j >= 2:
                        pe.wait_ge(m_act, p * EG + j - 1)
                    if kind == "D" and m == 0:
                        pe.wait_ge(m_alo, p * EG + j + 1)
                        if j == 0 and not first:
                            pe.wait_ge(m_out, p)
                    pe.wait_ge(lo_ready, p * NP + MOE0 + c + 1)
                    for k in range(2):
                        if kind == "G":
                            lhs = acts(2 * m + k, 0, P)
                            start, stop = (m == 0 and k == 0), (m == 3 and k == 1)
                        else:
                            i0 = (2 * m + k) * P
                            lhs = (a_hi[:, j % 2, i0:i0 + P], a_lo[:, j % 2, i0:i0 + P])
                            start, stop = (j == 0 and m == 0 and k == 0), (j == EG - 1 and m == 1 and k == 1)
                        for i in range(2):
                            bank = 2 * (j % 2) + i if kind == "G" else 4 + i
                            ins = product(ps[:, bank, :], lhs, weights(MOE0 + c, k * 1024 + i * 512, 512), start=start, stop=stop)
                    ins.then_inc(panel_used, 1)
                    if kind == "G" and m == 1:
                        if j >= 1:
                            turn(j - 1)
                        if j < 2 and not first:
                            scatter(p, 2 * j)
                    if kind == "G" and m == 3:
                        if j < 2 and not first:
                            scatter(p, 2 * j + 1)
                        if j == 2:
                            if first:
                                pe.wait_ge(m_glo, 1)
                            else:
                                pe.wait_ge(m_add, p * 4)
                            for t in range(TT):
                                ins = nc.tensor.transpose(ps[:, 7, t * P:(t + 1) * P], sel_f[:, t, :], ident[:])
                            ins.then_inc(m_selturn, 1)

            expert(0)
            with pe.Fori(1, E - 1) as p:
                expert(p)
            pe.wait_ge(info_ready, 1)
            extra = pe.value_load(info[0:1, 0:1], min_val=0, max_val=EXTRA)
            with pe.If(extra > 0):
                with pe.Fori(0, extra) as i:
                    expert(i + (E - 1))
            expert(extra + (E - 1), last=True)
            pe.wait_ge(m_selT, extra + E)
            for q in range(4):
                scatter(extra + E, q, bank=q)


_INS = ["x", "attn_norm", "ffn_norm", "hgrn_w_in", "hgrn_lb_logits", "hgrn_out_norm", "hgrn_w_o", "kv_norm",
        "w_kv", "moba_w_q", "moba_w_o", "ffn_w_gu", "ffn_w_down", "moe_router", "moe_w_gu", "moe_w_down", "final_norm"]


def kernel(**inputs):
    import concourse.bacc as bacc
    from concourse.bass_utils import run_bass_kernel_spmd

    nc = bacc.Bacc("TRN2", target_bir_lowering=False, num_devices=1)
    arrays, args = {}, []
    for name in _INS:
        a = np.ascontiguousarray(inputs[name])
        arrays[f"in_{name}"] = a
        args.append(nc.dram_tensor(f"in_{name}", a.shape, mybir.dt.from_np(a.dtype), kind="ExternalInput").ap())
    x = inputs["x"]
    args.append(nc.dram_tensor("out_0", x.shape, mybir.dt.from_np(np.dtype(x.dtype)), kind="ExternalOutput").ap())
    build_trunk(nc, *args)
    r = run_bass_kernel_spmd(nc, [arrays], core_ids=[0])
    return r.results[0]["out_0"]
```
